# Optimizing a Trainium2 kernel written in Bass

```python
import jax, jax.numpy as jnp
from jax import lax
import numpy as np

D_MODEL = 1024
BATCH = 1
SEQ = 512
DEPTH = 1
DEC_BATCH = 8
DEC_SEQ = 1
PAST_LEN = 256
PAGE_SIZE = 128

N_HEADS = 16
N_KV = 4
HEAD_DIM = 64
Q_PER_KV = N_HEADS // N_KV
NSA_WIDTH = N_HEADS * HEAD_DIM
KV_COLS = 2 * N_KV * HEAD_DIM
CMP_BLOCK = 64
SEL_BLOCK = CMP_BLOCK
N_SEL = 8
WINDOW = 512
Q_BLOCK = 64
SC_WIDTH = 512
SC_K = 3
LRU_WIDTH = 512
LRU_HEADS = 8
LRU_BW = LRU_WIDTH // LRU_HEADS
LRU_K = 4
LRU_C = 8.0
D_FF = -(-8 * D_MODEL // (3 * 256)) * 256

SPLIT_SIZES = (NSA_WIDTH, KV_COLS, KV_COLS, KV_COLS, 3 * N_HEADS,
               SC_WIDTH, SC_WIDTH, SC_WIDTH, LRU_WIDTH, LRU_WIDTH, 3 * D_MODEL)
SPLIT_POINTS = tuple(int(v) for v in np.cumsum(SPLIT_SIZES)[:-1])
N_IN = sum(SPLIT_SIZES)
SCALE = HEAD_DIM ** -0.5
EPS = 1e-6
NEG = -1e30
TINY = 1e-20
FORCE = 1e6

kernel_name = 'nsa_shortconv_rglru_hybrid_step'

def _rmsnorm(x, g):
    xf = x.astype(jnp.float32)
    y = xf * lax.rsqrt(jnp.mean(xf * xf, axis=-1, keepdims=True) + EPS)
    return (y * g.astype(jnp.float32)).astype(x.dtype)

def _masked_probs(s, mask):
    s = jnp.where(mask, s, NEG)
    m = jnp.max(s, axis=-1, keepdims=True)
    p = jnp.where(mask, jnp.exp(s - m), 0.0)
    return p / jnp.maximum(jnp.sum(p, axis=-1, keepdims=True), TINY)

def _compress(k, w):
    B, L, G, D = k.shape
    kb = k.reshape(B, L // CMP_BLOCK, CMP_BLOCK, G, D)
    return jnp.einsum('bnjgd,jd->bngd', kb, w)

def _to_blocks(k):
    B, L, G, D = k.shape
    return k.reshape(B, L // SEL_BLOCK, SEL_BLOCK, G, D).transpose(0, 3, 1, 2, 4)

def _cmp_and_select(qg, q_pos, k_c, v_c, w_ck, w_cv):
    kc = _compress(k_c, w_ck)
    vc = _compress(v_c, w_cv)
    nblk = kc.shape[1]
    s = jnp.einsum('btgrd,bngd->bgrtn', qg, kc).astype(jnp.float32) * SCALE
    blk = jnp.arange(nblk)
    mask = ((blk + 1) * CMP_BLOCK - 1)[None, :] <= q_pos[:, None]
    p = _masked_probs(s, mask)
    o = jnp.einsum('bgrtn,bngd->btgrd', p, vc)
    cur = (q_pos // SEL_BLOCK)[:, None]
    imp = jnp.sum(p, axis=2)
    imp = imp + FORCE * (blk == cur) + (0.5 * FORCE) * (blk == 0)[None, :]
    imp = jnp.where(blk[None, :] <= cur, imp, -FORCE)
    _, idx = lax.top_k(imp, min(N_SEL, nblk))
    return o, idx

def _sel_attn(qg, q_pos, idx, kb, vb):
    B, G, T, n = idx.shape
    M = n * SEL_BLOCK
    bi = jnp.arange(B)[:, None, None, None]
    gi = jnp.arange(G)[None, :, None, None]
    ks = kb[bi, gi, idx].reshape(B, G, T, M, HEAD_DIM)
    vs = vb[bi, gi, idx].reshape(B, G, T, M, HEAD_DIM)
    kpos = (idx[..., None] * SEL_BLOCK + jnp.arange(SEL_BLOCK)).reshape(B, G, T, M)[:, :, None]
    mask = kpos <= q_pos[:, None]
    s = jnp.einsum('btgrd,bgtmd->bgrtm', qg, ks).astype(jnp.float32) * SCALE
    p = _masked_probs(s, mask)
    return jnp.einsum('bgrtm,bgtmd->btgrd', p, vs)

def _win_attn(qg, q_pos, kw, vw, k_pos):
    s = jnp.einsum('btgrd,bkgd->bgrtk', qg, kw).astype(jnp.float32) * SCALE
    dlt = q_pos[:, None] - k_pos[None, :]
    mask = (dlt >= 0) & (dlt < WINDOW) & (k_pos >= 0)[None, :]
    p = _masked_probs(s, mask)
    return jnp.einsum('bgrtk,bkgd->btgrd', p, vw)

def _nsa_prompt(qg, pos, k_c, v_c, k_s, v_s, k_w, v_w, w_ck, w_cv):
    B, S, G, R, Dh = qg.shape
    o_c, idx = _cmp_and_select(qg, pos, k_c, v_c, w_ck, w_cv)
    kb, vb = _to_blocks(k_s), _to_blocks(v_s)
    pad = ((0, 0), (WINDOW, 0), (0, 0), (0, 0))
    kwp, vwp = jnp.pad(k_w, pad), jnp.pad(v_w, pad)
    span = WINDOW + Q_BLOCK

    def block(i):
        st = i * Q_BLOCK
        qb = lax.dynamic_slice_in_dim(qg, st, Q_BLOCK, axis=1)
        pb = st + jnp.arange(Q_BLOCK)
        ib = lax.dynamic_slice_in_dim(idx, st, Q_BLOCK, axis=2)
        o_s = _sel_attn(qb, pb, ib, kb, vb)
        kp = st - WINDOW + jnp.arange(span)
        o_w = _win_attn(qb, pb, lax.dynamic_slice_in_dim(kwp, st, span, axis=1),
                        lax.dynamic_slice_in_dim(vwp, st, span, axis=1), kp)
        return o_s, o_w

    o_s, o_w = lax.map(block, jnp.arange(S // Q_BLOCK))
    o_s = jnp.moveaxis(o_s, 0, 1).reshape(B, S, G, R, Dh)
    o_w = jnp.moveaxis(o_w, 0, 1).reshape(B, S, G, R, Dh)
    w_keep = min(WINDOW, S)
    win_state = jnp.stack([k_w[:, S - w_keep:], v_w[:, S - w_keep:]], axis=2)
    return o_c, o_s, o_w, win_state

def _make_nsa_sample(past, win_buf):
    def nsa_fn(qg, pos, k_c, v_c, k_s, v_s, k_w, v_w, w_ck, w_cv):
        T = qg.shape[1]
        P = past.shape[1]
        L = P + T
        pad = -(-L // CMP_BLOCK) * CMP_BLOCK - L

        def full(i, new):
            seq = jnp.concatenate([past[:, :, i], new], axis=1)
            return jnp.pad(seq, ((0, 0), (0, pad), (0, 0), (0, 0)))

        o_c, idx = _cmp_and_select(qg, pos, full(0, k_c), full(1, v_c), w_ck, w_cv)
        o_s = _sel_attn(qg, pos, idx, _to_blocks(full(2, k_s)), _to_blocks(full(3, v_s)))
        Wc = win_buf.shape[1]
        kw = jnp.concatenate([win_buf[:, :, 0], k_w], axis=1)
        vw = jnp.concatenate([win_buf[:, :, 1], v_w], axis=1)
        kp = (P - Wc) + jnp.arange(Wc + T)
        o_w = _win_attn(qg, pos, kw, vw, kp)
        win_state = jnp.stack([kw[:, T:], vw[:, T:]], axis=2)
        return o_c, o_s, o_w, win_state
    return nsa_fn

def _causal_conv(u, prev, w):
    K = w.shape[0]
    T = u.shape[1]
    ext = jnp.concatenate([prev.astype(u.dtype), u], axis=1)
    y = ext[:, 0:T] * w[0]
    for k in range(1, K):
        y = y + ext[:, k:k + T] * w[k]
    return y, ext[:, T:]

def _lru_step(hc, ab):
    a_t, b_t = ab
    hn = a_t * hc + b_t
    return hn, hn

def _layer_mixers(h, pos, lp, nsa_fn, sc_prev, lru_conv_prev, lru_h0):
    B, T, _ = h.shape
    (q, kv_c, kv_s, kv_w, g_nsa, b_sc, c_sc, x_sc, x_lru, y_lru, g_mix) = jnp.split(
        h @ lp['w_in'], SPLIT_POINTS, axis=-1)
    qg = q.reshape(B, T, N_KV, Q_PER_KV, HEAD_DIM)
    kv_c = kv_c.reshape(B, T, 2, N_KV, HEAD_DIM)
    kv_s = kv_s.reshape(B, T, 2, N_KV, HEAD_DIM)
    kv_w = kv_w.reshape(B, T, 2, N_KV, HEAD_DIM)
    o_c, o_s, o_w, win_state = nsa_fn(qg, pos, kv_c[:, :, 0], kv_c[:, :, 1], kv_s[:, :, 0], kv_s[:, :, 1],
                                      kv_w[:, :, 0], kv_w[:, :, 1], lp['w_cmp_k'], lp['w_cmp_v'])
    g = jax.nn.sigmoid(g_nsa.reshape(B, T, N_KV, Q_PER_KV, 3, 1))
    o_nsa = (g[..., 0, :] * o_c + g[..., 1, :] * o_s + g[..., 2, :] * o_w).reshape(B, T, NSA_WIDTH)
    u_nsa = o_nsa @ lp['w_nsa_out']
    conv_u, sc_state = _causal_conv(c_sc * x_sc, sc_prev, lp['w_sc_conv'])
    u_sc = (b_sc * conv_u) @ lp['w_sc_out']
    xc, lru_conv_state = _causal_conv(x_lru, lru_conv_prev, lp['w_lru_conv'])
    xc = xc + lp['b_lru_conv']
    gates = jnp.einsum('bthi,khij->kbthj', xc.reshape(B, T, LRU_HEADS, LRU_BW),
                       lp['w_lru_gate']).reshape(2, B, T, LRU_WIDTH) + lp['b_lru_gate'][:, None, None, :]
    gates = jax.nn.sigmoid(gates.astype(jnp.float32))
    log_a = -LRU_C * gates[0] * jax.nn.softplus(-lp['lru_lambda'].astype(jnp.float32))
    reset = (pos == 0)[None, :, None]
    a = jnp.where(reset, 0.0, jnp.exp(log_a))
    mult = jnp.where(reset, 1.0, jnp.sqrt(-jnp.expm1(2.0 * log_a)))
    bx = mult * gates[1] * xc.astype(jnp.float32)
    h_last, hs = lax.scan(_lru_step, lru_h0.astype(jnp.float32),
                          (jnp.swapaxes(a, 0, 1), jnp.swapaxes(bx, 0, 1)))
    hs = jnp.swapaxes(hs, 0, 1).astype(h.dtype)
    u_lru = (hs * jax.nn.gelu(y_lru)) @ lp['w_lru_out']
    gm = jax.nn.sigmoid(g_mix.reshape(B, T, 3, D_MODEL))
    out = (gm[:, :, 0] * u_nsa + gm[:, :, 1] * u_sc + gm[:, :, 2] * u_lru) @ lp['w_o']
    kv_rows = jnp.concatenate([kv_c, kv_s], axis=2)
    return out, (kv_rows, win_state, sc_state, lru_conv_state, h_last)

def _swiglu(h, w_in, w_out):
    gt, up = jnp.split(h @ w_in, 2, axis=-1)
    return (jax.nn.silu(gt) * up) @ w_out

def _stack_states(states):
    return tuple(jnp.stack([s[i] for s in states]) for i in range(5))

def setup_inputs(seed: int = 0) -> dict:
    key = jax.random.key(seed)
    k = jax.random.split(key, 32)
    f32 = jnp.float32

    def nrm(kk, shape, fan):
        return jax.random.normal(kk, shape, f32) * (fan ** -0.5)

    n_pages = PAST_LEN // PAGE_SIZE
    n_used = DEC_BATCH * n_pages
    n_pool = n_used + max(1, n_used // 4)
    win_len = min(WINDOW, PAST_LEN)
    page_table = jax.random.permutation(k[0], n_pool)[:n_used].reshape(DEC_BATCH, n_pages).astype(jnp.int32)
    u = jax.random.uniform(k[1], (DEPTH, LRU_WIDTH), f32, 0.9, 0.999)
    return {
        'x_prompt': jax.random.normal(k[2], (BATCH, SEQ, D_MODEL), f32),
        'x_sample': jax.random.normal(k[3], (DEC_BATCH, DEC_SEQ, D_MODEL), f32),
        'cache_kv': jax.random.normal(k[4], (DEPTH, n_pool, PAGE_SIZE, 4, N_KV, HEAD_DIM), f32),
        'cache_win': jax.random.normal(k[5], (DEPTH, DEC_BATCH, win_len, 2, N_KV, HEAD_DIM), f32),
        'state_sconv': jax.random.normal(k[6], (DEPTH, DEC_BATCH, SC_K - 1, SC_WIDTH), f32),
        'state_lru_conv': jax.random.normal(k[7], (DEPTH, DEC_BATCH, LRU_K - 1, LRU_WIDTH), f32),
        'state_lru_h': 0.5 * jax.random.normal(k[8], (DEPTH, DEC_BATCH, LRU_WIDTH), f32),
        'page_table': page_table,
        'norm1_g': 1.0 + 0.1 * jax.random.normal(k[9], (DEPTH, D_MODEL), f32),
        'w_in': nrm(k[10], (DEPTH, D_MODEL, N_IN), D_MODEL),
        'w_cmp_k': (1.0 + 0.1 * jax.random.normal(k[11], (DEPTH, CMP_BLOCK, HEAD_DIM), f32)) * CMP_BLOCK ** -0.5,
        'w_cmp_v': (1.0 + 0.1 * jax.random.normal(k[12], (DEPTH, CMP_BLOCK, HEAD_DIM), f32)) * CMP_BLOCK ** -0.5,
        'w_nsa_out': nrm(k[13], (DEPTH, NSA_WIDTH, D_MODEL), NSA_WIDTH),
        'w_sc_conv': nrm(k[14], (DEPTH, SC_K, SC_WIDTH), SC_K),
        'w_sc_out': nrm(k[15], (DEPTH, SC_WIDTH, D_MODEL), SC_WIDTH),
        'w_lru_conv': nrm(k[16], (DEPTH, LRU_K, LRU_WIDTH), LRU_K),
        'b_lru_conv': 0.01 * jax.random.normal(k[17], (DEPTH, LRU_WIDTH), f32),
        'w_lru_gate': nrm(k[18], (DEPTH, 2, LRU_HEADS, LRU_BW, LRU_BW), LRU_BW),
        'b_lru_gate': 0.01 * jax.random.normal(k[19], (DEPTH, 2, LRU_WIDTH), f32),
        'lru_lambda': jnp.log(u / (1.0 - u)),
        'w_lru_out': nrm(k[20], (DEPTH, LRU_WIDTH, D_MODEL), LRU_WIDTH),
        'w_o': nrm(k[21], (DEPTH, D_MODEL, D_MODEL), D_MODEL),
        'norm2_g': 1.0 + 0.1 * jax.random.normal(k[22], (DEPTH, D_MODEL), f32),
        'w_ffn_in': nrm(k[23], (DEPTH, D_MODEL, 2 * D_FF), D_MODEL),
        'w_ffn_out': nrm(k[24], (DEPTH, D_FF, D_MODEL), D_FF),
        'final_g': 1.0 + 0.1 * jax.random.normal(k[25], (D_MODEL,), f32),
    }

def reference(x_prompt, x_sample, cache_kv, cache_win, state_sconv, state_lru_conv, state_lru_h, page_table,
              norm1_g, w_in, w_cmp_k, w_cmp_v, w_nsa_out, w_sc_conv, w_sc_out, w_lru_conv, b_lru_conv,
              w_lru_gate, b_lru_gate, lru_lambda, w_lru_out, w_o, norm2_g, w_ffn_in, w_ffn_out, final_g):
    B, S, _ = x_prompt.shape
    DB, T, _ = x_sample.shape
    P = page_table.shape[1] * cache_kv.shape[2]
    pos_p = jnp.arange(S, dtype=jnp.int32)
    pos_s = P + jnp.arange(T, dtype=jnp.int32)
    xp, xs = x_prompt, x_sample
    st_p, st_s = [], []
    for l in range(DEPTH):
        lp = {'w_in': w_in[l], 'w_cmp_k': w_cmp_k[l], 'w_cmp_v': w_cmp_v[l], 'w_nsa_out': w_nsa_out[l],
              'w_sc_conv': w_sc_conv[l], 'w_sc_out': w_sc_out[l], 'w_lru_conv': w_lru_conv[l],
              'b_lru_conv': b_lru_conv[l], 'w_lru_gate': w_lru_gate[l], 'b_lru_gate': b_lru_gate[l],
              'lru_lambda': lru_lambda[l], 'w_lru_out': w_lru_out[l], 'w_o': w_o[l]}
        mp, sp = _layer_mixers(_rmsnorm(xp, norm1_g[l]), pos_p, lp, _nsa_prompt,
                               jnp.zeros((B, SC_K - 1, SC_WIDTH), xp.dtype),
                               jnp.zeros((B, LRU_K - 1, LRU_WIDTH), xp.dtype),
                               jnp.zeros((B, LRU_WIDTH), jnp.float32))
        xp = xp + mp
        xp = xp + _swiglu(_rmsnorm(xp, norm2_g[l]), w_ffn_in[l], w_ffn_out[l])
        past = cache_kv[l][page_table].reshape(DB, P, 4, N_KV, HEAD_DIM)
        ms, ss = _layer_mixers(_rmsnorm(xs, norm1_g[l]), pos_s, lp, _make_nsa_sample(past, cache_win[l]),
                               state_sconv[l], state_lru_conv[l], state_lru_h[l])
        xs = xs + ms
        xs = xs + _swiglu(_rmsnorm(xs, norm2_g[l]), w_ffn_in[l], w_ffn_out[l])
        st_p.append(sp)
        st_s.append(ss)
    y_prompt = _rmsnorm(xp, final_g)
    y_sample = _rmsnorm(xs, final_g)
    kv_p, win_p, sc_p, lc_p, lh_p = _stack_states(st_p)
    kv_s, win_s, sc_s, lc_s, lh_s = _stack_states(st_s)
    return (y_prompt, y_sample, kv_p, win_p, sc_p, lc_p, lh_p, kv_s, win_s, sc_s, lc_s, lh_s)


_drawn_inputs = setup_inputs


def setup_inputs(seed=0):
    import zlib

    import numpy as np

    out = dict(_drawn_inputs(seed))
    spreads = {}
    factors = {'w_cmp_k': 5.233, 'w_cmp_v': 3.234, 'b_lru_gate': 8.0}
    for name, (base, spread) in spreads.items():
        noise = np.random.default_rng([zlib.crc32(name.encode()), seed]).standard_normal(out[name].shape)
        drawn = base * np.exp(spread * noise) if base else spread * noise
        out[name] = __import__('jax').numpy.asarray(drawn.astype(out[name].dtype))
    for name, factor in factors.items():
        out[name] = (out[name] * factor).astype(out[name].dtype)
    return out
```

```python
from contextlib import ExitStack

import concourse.bass as bass
from concourse import mybir

F32 = mybir.dt.float32
F32R = mybir.dt.float32r
I32 = mybir.dt.int32
ACT = mybir.ActivationFunctionType
ALU = mybir.AluOpType
AX = mybir.AxisListType

P = 128
D_MODEL = 1024
SEQ = 512
NS = 8
T = SEQ + NS
HALF = T // 2
KT = D_MODEL // P
QT = SEQ // P
N_HEADS, N_KV, DH = 16, 4, 64
R = N_HEADS // N_KV
PAST, PAGE = 256, 128
NPG = PAST // PAGE
CMP = 64
NBLK = SEQ // CMP
NBLK_S = PAST // CMP
KVC = N_KV * DH
WID = 512
WT = WID // P
D_FF = 2816
FT = D_FF // P
CW = 256
CHUNK = KT * CW
SCALE = DH ** -0.5
EPS = 1e-6
NEG = -1e30
TINY = 1e-20
GELU_C = 0.7978845608028654

COL_Q, COL_KV, COL_G = 0, 1024, 2560
COL_B, COL_C, COL_X, COL_XL, COL_YL, COL_GM = 2608, 3120, 3632, 4144, 4656, 5168

C_XL, C_C, C_X, C_B, C_YL, C_MIX1, C_MIX2 = 0, 2, 4, 6, 8, 10, 18
C_Q, C_KV, C_GM0, C_NSA, C_WO, C_FI, C_FO, C_END = 26, 30, 36, 40, 44, 48, 70, 82
STATE_OUTS = 6 + 3 * QT + 3
TABLES = 19

V_WSC, V_WLRU, V_BLRU, V_BGATE, V_LAM, V_SSC, V_SLC, V_SH, V_ROWS = 0, 3, 7, 8, 10, 11, 27, 51, 59


def build(nc, x_prompt, x_sample, cache_kv, cache_win, state_sconv, state_lru_conv, state_lru_h, page_table,
          norm1_g, w_in, w_cmp_k, w_cmp_v, w_nsa_out, w_sc_conv, w_sc_out, w_lru_conv, b_lru_conv, w_lru_gate,
          b_lru_gate, lru_lambda, w_lru_out, w_o, norm2_g, w_ffn_in, w_ffn_out, final_g,
          y_prompt, y_sample, kv_p, win_p, sconv_p, lruconv_p, lruh_p, kv_s, win_s, sconv_s, lruconv_s, lruh_s):
    n_pool = cache_kv.shape[1]
    with ExitStack() as ctx:
        def sem(name):
            return ctx.enter_context(nc.semaphore(name))

        base = (nc.sbuf_base + 31) // 32 * 32
        end = nc.sbuf_usable_end // 32 * 32

        def size(shape):
            n = 4
            for s in shape[1:]:
                n *= s
            return (n + 31) // 32 * 32

        class Region:
            def __init__(self, off, end):
                self.off, self.end = off, end

            def __call__(self, name, shape, dt=F32):
                o = self.off
                self.off += size(shape)
                assert self.off <= self.end, (name, self.off - self.end)
                return nc.alloc_sbuf_tensor_at(name, shape, dt, offset=o)

        sb = Region(base, end)
        xT = sb("xT", [P, KT, T])
        raw = [sb(f"w_raw{b}", [P, CHUNK]) for b in range(2)]
        wh = [sb(f"w_hi{b}", [P, CHUNK], F32R) for b in range(2)]
        wl = [sb(f"w_lo{b}", [P, CHUNK], F32R) for b in range(2)]
        th = sb("th", [P, 2, T])
        tmp = sb("tmp", [P, 2, T])
        rstd = sb("rstd", [P, T])
        ident = sb("ident", [P, P])
        ones = sb("ones", [P, P])
        ident_r = sb("ident_r", [P, P], F32R)
        causal_r = sb("causal_r", [P, P], F32R)
        g_cols = sb("g_cols", [P, 3, KT])
        wcT = sb("wcT", [P, 2, CMP])
        wc_tok = sb("wc_tok", [P, 2, DH])
        cmask = sb("cmask", [P, QT, 1, NBLK])
        cmask01 = sb("cmask01", [P, QT, 1, NBLK])
        headmask = sb("headmask", [P, N_HEADS])
        rep = sb("rep", [NBLK, N_HEADS, NBLK])
        seqmask = sb("seqmask", [P, NS])
        offseq = sb("offseq", [P, NS])
        gmask3 = sb("gmask3", [P, NS, N_KV])
        gmask = sb("gmask", [P, N_KV])
        blkpad = sb("blkpad", [P, NPG, NBLK_S])
        eps_col = sb("eps_col", [P, 1])
        pages = sb("pages", [1, NS * NPG], I32)
        smalls = sb("smalls", [P, 6, N_HEADS * QT])
        gates_s = sb("gates_s", [P, 3])
        gates_tok = sb("gates_tok", [P, QT, 3 * N_HEADS])
        gates_stok = sb("gates_stok", [NS, 3 * N_HEADS])
        h_off = sb.off
        hH = sb("hH", [P, KT, T], F32R)
        hL = sb("hL", [P, KT, T], F32R)
        rest = sb.off
        acc_off = end - size([P, KT, T])
        acc = nc.alloc_sbuf_tensor_at("acc", [P, KT, T], F32, offset=acc_off)

        era = Region(rest, end)
        vecs = era("vecs", [V_ROWS, WID])
        vecT = era("vecT", [P, WT, V_ROWS])
        wg = era("wg", [P, 2, WT, P])
        spl = era("spl", [P, 11, WT])
        hb = era("hb", [P, WT, 2])
        eraA_off = era.off
        xc = era("xc", [P, WT, T])
        t1 = era("t1", [P, WT, T])
        t0 = era("t0", [P, WT, T])
        la = era("la", [P, WT, T])
        lm = era("lm", [P, WT, T])
        cb = era("cb", [P, WT, T])
        vH = era("vH", [P, WT, T], F32R)
        vL = era("vL", [P, WT, T], F32R)
        exl = era("exl", [P, WT, 3 + T])
        eu = era("eu", [P, WT, 2 + T])
        over = Region(eraA_off, end)
        lrH = over("lrH", [P, WT, T], F32R)
        lrL = over("lrL", [P, WT, T], F32R)
        over = Region(rest, eraA_off)
        st_u = over("st_u", [2 + NS, WID])
        over = Region(eraA_off - size([P, WT, 2]) - size([P, 11, WT]) - size([P, 2, WT, P]), eraA_off)
        st_x = over("st_x", [3 + NS, WID])
        st_h = over("st_h", [1 + NS, WID])
        over = Region(eraA_off, acc_off)
        x_in = over("x_in", [P, QT, D_MODEL])
        xs_in = over("xs_in", [NS, D_MODEL])
        g_rows = over("g_rows", [3 * KT, P])
        wc_rows = over("wc_rows", [CMP, 2, 2, DH])

        era = Region(rest, acc_off)
        qT = era("qT", [P, KT, T])
        kT = era("kT", [P, 4, T])
        kv_tok = era("kv_tok", [P, QT, 4, KVC])
        kvs_tok = era("kvs_tok", [NS, 4, KVC])
        vt_off = era.off
        vT = era("vT", [P, 8, T])
        th0 = era("th0", [P, KT, T])
        over = Region(vt_off, vt_off + size([P, 8, T]))
        onsa = over("onsa", [P, QT, D_MODEL])
        over = Region(rest + size([P, KT, T]) + size([P, 4, T]), vt_off)
        wt_raw = over("wt_raw", [P, KT, P])
        wtH = over("wtH", [P, KT, P], F32R)
        wtL = over("wtL", [P, KT, P], F32R)
        over = Region(h_off, rest)
        q_st = [[over(f"q_st{b}", [P, SEQ])[:, :] for b in range(2)], [th[:, b, 0:SEQ] for b in range(2)]]
        k_st = [[over(f"k_st{b}", [P, SEQ])[:, :] for b in range(2)], [rstd[:, 0:SEQ], tmp[:, 1, 0:SEQ]]]
        p_off = over.off
        prob = [over(f"prob{b}", [P, SEQ]) for b in range(4)]
        probT = [over(f"probT{b}", [P, QT, P]) for b in range(2)]
        kvc_tok = over("kvc_tok", [P, QT, 2, KVC])
        kvcs_tok = over("kvcs_tok", [NS, 2, KVC])
        asum = over("asum", [P, 4, QT])
        anm = over("anm", [P, 8])
        acf = over("acf", [P, 2, QT])
        over = Region(p_off, p_off + 6 * 2048)
        vbig = over("vbig", [P, D_MODEL])
        pcT = over("pcT", [P, QT, P])

        over = Region(h_off, rest)
        QSTEP, PSTEP = 2 * P + N_HEADS, P + N_HEADS
        q_padf = over("q_pad", [P, NS * QSTEP + P + 3 * R])
        q_pad = q_padf[:, 0:NS * 2 * P].rearrange("p (s f c) -> p s f c", s=NS, f=2)
        q_all = over("q_all", [P, 2, P])
        pT_padf = over("pT_pad", [P, (NPG - 1) * NS * P + NS * PSTEP])
        pT_pad = pT_padf[:, 0:NPG * NS * P].rearrange("p (g s c) -> p g s c", g=NPG, s=NS)
        kTs = [over(f"kTs{b}", [P, 2, PAST]) for b in range(2)]
        s_sb = th[:, 1, 0:PAST + NS]
        p_sb = rstd[:, 0:PAST + NS]
        pT_new = over("pT_new", [NS, P])
        pT_cmpf = over("pT_cmp", [NBLK_S, NS * PSTEP])
        pT_cmp = pT_cmpf[:, 0:NS * P].rearrange("p (s c) -> p s c", s=NS)
        kcs = over("kcs", [P, NS, 2, NBLK_S])
        o_all = tmp[:, 0, 0:KVC].rearrange("p (g d) -> p g d", g=N_KV)
        o_sel = tmp[:, 1, 0:DH]
        o_sum = th[:, 0, 0:2 * DH]
        over = Region(rest, rest + size([P, KT, T]))
        prod = [over(f"prod{b}", [P, NPG, N_KV, DH]) for b in range(2)]
        vcs = over("vcs", [NBLK_S, NS, KVC])
        over = Region(rest + size([P, KT, T]) + size([P, 4, T]), vt_off)
        slot = [over(f"slot{s}", [P, NPG, KVC]) for s in range(NS)]
        over = Region(rest, vt_off)
        onH = over("onH", [P, KT, T], F32R)
        onL = over("onL", [P, KT, T], F32R)

        era = Region(rest, end)
        actH = era("actH", [P, FT, T], F32R)
        actL = era("actL", [P, FT, T], F32R)
        over = Region(rest, end)
        y_tok = [over(f"y_tok{q}", [P, D_MODEL]) for q in range(QT)]
        ys_tok = over("ys_tok", [NS, D_MODEL])
        yT = over("yT", [P, KT, T])

        D = [ctx.enter_context(nc.psum_tensor(f"D{m}", [P, 2, 512], F32)) for m in range(2)]
        E = ctx.enter_context(nc.psum_tensor("E", [P, 4, 512], F32))

        kc_sum = smalls[:, 5, 0:32].rearrange("p (n k) -> p n k", n=4)
        kc_blk = smalls[:, 4, 0:32].rearrange("p (f c) -> p f c", f=2)

        x_landed = [sem(f"x_landed{q}") for q in range(QT)]
        xs_landed = sem("xs_landed")
        tables_landed = sem("tables_landed")
        wg_landed = sem("wg_landed")
        gcols_landed = sem("gcols_landed")
        raw_landed = [sem(f"raw_landed{b}") for b in range(2)]
        pages_landed = sem("pages_landed")
        slot_landed = [sem(f"slot_landed{s}") for s in range(NS)]
        gates_s_landed = sem("gates_s_landed")
        out_written = sem("out_written")
        rows_moved = sem("rows_moved")
        pool_step = sem("pool_step")
        consts_ready = sem("consts_ready")
        hi_done = sem("hi_done")
        lo_done = sem("lo_done")
        pe_done = sem("pe_done")
        tile_free = [sem(f"tile_free{m}") for m in range(2)]
        x_turned = sem("x_turned")
        x_evac = sem("x_evac")
        tables_turned = sem("tables_turned")
        tables_evac = sem("tables_evac")
        sq_done = sem("sq_done")
        sq_summed = sem("sq_summed")
        rms_done = sem("rms_done")
        rstd_done = sem("rstd_done")
        normed = sem("normed")
        norm_hi = sem("norm_hi")
        norm_lo = sem("norm_lo")
        hb_ready = sem("hb_ready")
        lam_abs = sem("lam_abs")
        lam_exp = sem("lam_exp")
        vec_step = sem("vec_step")
        xc_ready = sem("xc_ready")
        cx_ready = sem("cx_ready")
        gate_mm = sem("gate_mm")
        gate_tanh = sem("gate_tanh")
        v_hi = sem("v_hi")
        v_lo = sem("v_lo")
        neg_la = sem("neg_la")
        la_exp = sem("la_exp")
        la_tanh = sem("la_tanh")
        mult_sq = sem("mult_sq")
        mult_ready = sem("mult_ready")
        y_sq = sem("y_sq")
        gelu_arg = sem("gelu_arg")
        gelu_tanh = sem("gelu_tanh")
        lr_prod = sem("lr_prod")
        lr_hi = sem("lr_hi")
        lr_lo = sem("lr_lo")
        h_ready = sem("h_ready")
        tails_turned = sem("tails_turned")
        tails_evac = sem("tails_evac")
        mixed = sem("mixed")
        wt_hi = sem("wt_hi")
        wt_lo = sem("wt_lo")
        gnsa_mm = sem("gnsa_mm")
        q_even = sem("q_even")
        gnsa_tanh = sem("gnsa_tanh")
        gnsa_turned = sem("gnsa_turned")
        gates_ready = sem("gates_ready")
        cmp_sums = sem("cmp_sums")
        vc_turned = sem("vc_turned")
        vc_evac = sem("vc_evac")
        vc_rep = sem("vc_rep")
        vbig_ready = sem("vbig_ready")
        cmp_scores = sem("cmp_scores")
        cmp_shift = sem("cmp_shift")
        cmp_exp = sem("cmp_exp")
        cmp_prob = sem("cmp_prob")
        kv_turned = sem("kv_turned")
        kv_evac = sem("kv_evac")
        kvs_evac = sem("kvs_evac")
        pc_turned = sem("pc_turned")
        pc_evac = sem("pc_evac")
        cmp_out = sem("cmp_out")
        cmp_evac = sem("cmp_evac")
        staged = sem("staged")
        scores_done = sem("scores_done")
        nmax_done = sem("nmax_done")
        exp_done = sem("exp_done")
        probs_turned = sem("probs_turned")
        probT_done = sem("probT_done")
        pv_done = sem("pv_done")
        o_added = sem("o_added")
        att_step = sem("att_step")
        qpad_ready = sem("qpad_ready")
        s_prod = sem("s_prod")
        s_kc_mm = sem("s_kc_mm")
        s_kc_evac = sem("s_kc_evac")
        s_vc_mm = sem("s_vc_mm")
        s_vc_evac = sem("s_vc_evac")
        s_k_turned = sem("s_k_turned")
        s_k_evac = sem("s_k_evac")
        s_k_used = sem("s_k_used")
        s_scores = sem("s_scores")
        s_nmax = sem("s_nmax")
        s_exp = sem("s_exp")
        s_p_turned = sem("s_p_turned")
        s_pT = sem("s_pT")
        s_v_used = sem("s_v_used")
        s_out = sem("s_out")
        s_sel = sem("s_sel")
        os_turned = sem("os_turned")
        on_turned = sem("on_turned")
        on_hi = sem("on_hi")
        on_lo = sem("on_lo")
        ons_hi = sem("ons_hi")
        ons_lo = sem("ons_lo")
        mix_sum = sem("mix_sum")
        mix_hi = sem("mix_hi")
        mix_lo = sem("mix_lo")
        ffn_tanh = sem("ffn_tanh")
        act_hi = sem("act_hi")
        act_lo = sem("act_lo")
        x_last = sem("x_last")
        y_ready = sem("y_ready")
        y_turned = sem("y_turned")
        y_evac_a = sem("y_evac_a")
        y_evac_v = sem("y_evac_v")

        block = ctx.enter_context(nc.Block())

        w_in_k = w_in[0].rearrange("(kt p) n -> p kt n", p=P)

        @block.sync
        def _(sp):
            outs = [0]

            def out(dst, src):
                sp.dma_start(dst, src).then_inc(out_written, 16)
                outs[0] += 16

            def load(c, b, src, nk=KT, fresh=False):
                if not fresh:
                    sp.wait_ge(lo_done, 2 * c - 2)
                dst = raw[b][:, 0:nk * CW].rearrange("p (k n) -> p k n", k=nk)
                for k in (slice(0, nk // 2), slice(nk // 2, nk)):
                    sp.dma_start(dst[:, k, :], src[:, k, :]).then_inc(raw_landed[b], 16)

            def load_pair(c, col, fresh=False):
                for b in range(2):
                    load(c + b, b, w_in_k[:, :, bass.ds(col + b * CW, CW)], fresh=fresh)

            for q in range(QT):
                sp.dma_start(x_in[:, q, :], x_prompt[0, q * P:(q + 1) * P, :]).then_inc(x_landed[q], 16)
            load_pair(C_XL, COL_XL, fresh=True)
            for c, col in ((C_C, COL_C), (C_X, COL_X), (C_B, COL_B), (C_YL, COL_YL)):
                load_pair(c, col)
            for c, gate, w in ((C_MIX1, 1, w_sc_out), (C_MIX2, 2, w_lru_out)):
                wk = w[0].rearrange("(kt p) n -> p kt n", p=P)
                if c == C_MIX2:
                    sp.wait_ge(tails_evac, 2)
                    out(sconv_p[0, 0], st_u[0:2, :])
                    out(sconv_s[0, :, 1, :], st_u[2:2 + NS, :])
                    out(lruconv_p[0, 0], st_x[0:3, :])
                    out(lruconv_s[0, :, 2, :], st_x[3:3 + NS, :])
                with sp.Fori(1, 5) as i:
                    load(c - 2 + 2 * i, 0, w_in_k[:, :, bass.ds(COL_GM + gate * D_MODEL - CW + i * CW, CW)])
                    load(c - 1 + 2 * i, 1, wk[:, :, bass.ds(i * CW - CW, CW)], WT)
            sp.wait_ge(tails_evac, 3)
            out(lruh_p[0], st_h[0:1, :])
            out(lruh_s[0], st_h[1:1 + NS, :])
            with sp.Fori(0, 2) as i:
                load_pair(C_Q + 2 * i, COL_Q + i * 2 * CW)
            with sp.Fori(0, 3) as i:
                load_pair(C_KV + 2 * i, COL_KV + i * 2 * CW)
            with sp.Fori(0, 2) as i:
                load_pair(C_GM0 + 2 * i, COL_GM + i * 2 * CW)
            wk = w_nsa_out[0].rearrange("(kt p) n -> p kt n", p=P)
            for b in range(2):
                load(C_NSA + b, b, wk[:, :, b * CW:(b + 1) * CW])
            sp.wait_ge(gates_ready, 2)
            for s in range(NS):
                sp.dma_start(gates_s[s * N_HEADS:(s + 1) * N_HEADS, :], gates_stok[s:s + 1, :])\
                    .then_inc(gates_s_landed, 16)
            sp.wait_ge(kv_evac, 12)
            sp.wait_ge(kvs_evac, 3)
            kvp = kv_p[0, 0].rearrange("(q p) c g d -> p q c (g d)", p=P)
            wnp = win_p[0, 0].rearrange("(q p) c g d -> p q c (g d)", p=P)
            for q in range(QT):
                out(kvp[:, q, 0:2, :], kvc_tok[:, q, :, :])
                out(kvp[:, q, 2:4, :], kv_tok[:, q, 0:2, :])
                out(wnp[:, q, :, :], kv_tok[:, q, 2:4, :])
            kvs = kv_s[0, :, 0].rearrange("s c g d -> s c (g d)")
            out(kvs[:, 0:2, :], kvcs_tok[:, :, :])
            out(kvs[:, 2:4, :], kvs_tok[:, 0:2, :])
            out(win_s[0, :, PAST - 1].rearrange("s c g d -> s c (g d)"), kvs_tok[:, 2:4, :])
            assert outs[0] == 16 * STATE_OUTS
            sp.wait_ge(out_written, 16 * STATE_OUTS)
            sp.wait_ge(pv_done, 2 + 128)
            sp.wait_ge(pages_landed, 16)
            page = [[sp.value_load(pages[0:1, s * NPG + g:s * NPG + g + 1], min_val=0, max_val=n_pool - 1)
                     for g in range(NPG)] for s in range(NS)]
            pool = cache_kv[0].rearrange("n t c g d -> n t c (g d)")
            for y in range(3):
                for v in range(2):
                    for s in range(NS):
                        if y == 0 and v == 1:
                            sp.wait_ge(s_prod, s + 1)
                        elif y == 1 and v == 0:
                            sp.wait_ge(s_prod, NS + s + 1)
                        elif y > 0 and v == 1:
                            sp.wait_ge(s_k_turned, (y - 1) * NS + s + 1)
                        elif y == 2 and s < NS - 1:
                            sp.wait_ge(s_v_used, s + 1)
                        elif y == 2:
                            sp.wait_ge(s_out, 2)
                        if y < 2:
                            for g in range(NPG):
                                src = pool[bass.ds(page[s][g], 1), :, 2 * y + v, :]
                                sp.dma_start(slot[s][:, g, :], src.rearrange("n t x -> (n t) x"))\
                                    .then_inc(slot_landed[s], 16)
                        else:
                            src = cache_win[0, s, :, v].rearrange("(g t) h d -> t g (h d)", t=PAGE)
                            sp.dma_start(slot[s][:, :, :], src).then_inc(slot_landed[s], 16)
            for b in range(2):
                load(C_NSA + 2 + b, b, wk[:, :, (2 + b) * CW:(3 + b) * CW])
            wk = w_o[0].rearrange("(kt p) n -> p kt n", p=P)
            with sp.Fori(0, 2) as i:
                for b in range(2):
                    load(C_WO + 2 * i + b, b, wk[:, :, bass.ds(i * 2 * CW + b * CW, CW)])
            wk = w_ffn_in[0].rearrange("(kt p) n -> p kt n", p=P)
            with sp.Fori(0, D_FF // CW) as i:
                for b in range(2):
                    load(C_FI + 2 * i + b, b, wk[:, :, bass.ds(i * CW + b * D_FF, CW)])
            wk = w_ffn_out[0].rearrange("(kt p) n -> p kt n", p=P)
            with sp.Fori(0, 2) as i:
                for j in range(6):
                    k0, nk = ((0, KT), (KT, KT), (2 * KT, FT - 2 * KT))[j % 3]
                    load(C_FO + 6 * i + j, j % 2, wk[:, k0:k0 + nk, bass.ds(i * 2 * CW + (j // 3) * CW, CW)], nk)
            for q in range(QT):
                sp.wait_ge(y_evac_a, q + 1)
                sp.wait_ge(y_evac_v, q + 1)
                out(y_prompt[0, q * P:(q + 1) * P, :], y_tok[q][:, :])
            sp.wait_ge(y_evac_v, QT + 2)
            out(y_sample[:, 0, :], ys_tok[:, :])
            sp.wait_ge(out_written, outs[0])
            sp.wait_ge(rows_moved, 3 * 16)

        @block.gpsimd
        def _(pool):
            n = [0]

            def step(ins):
                ins.then_inc(pool_step, 1)
                n[0] += 1

            def settle():
                pool.wait_ge(pool_step, n[0])

            def fill_where(ap, op, fill, base_, chan, pattern):
                step(nc.gpsimd.affine_select(out=ap, in_=ap, compare_op=op, fill=fill, base=base_, pattern=pattern,
                                             channel_multiplier=chan))

            step(nc.gpsimd.memset(ident[:, :], 0.0))
            step(nc.gpsimd.memset(ones[:, :], 1.0 / D_MODEL))
            step(nc.gpsimd.memset(tmp[:, 0, 0:P], 0.0))
            step(nc.gpsimd.memset(wg[:, :, :, :], 0.0))
            step(nc.gpsimd.memset(cmask[:, :, :, :], 0.0))
            step(nc.gpsimd.memset(cmask01[:, :, :, :], 1.0))
            step(nc.gpsimd.memset(headmask[:, :], 1.0))
            step(nc.gpsimd.memset(rep[:, :, :], 0.0))
            step(nc.gpsimd.memset(seqmask[:, :], 1.0))
            step(nc.gpsimd.memset(gmask3[:, :, :], 1.0))
            step(nc.gpsimd.memset(blkpad[:, :, :], 0.0))
            step(nc.gpsimd.memset(smalls[:, :, :], 0.0))
            step(nc.gpsimd.memset(eps_col[:, :], EPS))
            step(nc.gpsimd.memset(exl[:, :, 0:3], 0.0))
            step(nc.gpsimd.memset(eu[:, :, 0:2], 0.0))
            settle()
            fill_where(ident[:, :], ALU.not_equal, 1.0, 0, 1, [[-1, P]])
            fill_where(tmp[:, 0, 0:P], ALU.is_ge, NEG, 0, 1, [[-1, P]])
            whole = [[P, QT], [0, 1], [-CMP, NBLK]]
            fill_where(cmask[:, :, :, :], ALU.is_ge, NEG, 1 - CMP, 1, whole)
            fill_where(cmask01[:, :, :, :], ALU.is_ge, 0.0, 1 - CMP, 1, whole)
            fill_where(headmask[:, :], ALU.is_ge, 0.0, 0, 1, [[-NBLK, N_HEADS]])
            fill_where(rep[:, :, :], ALU.not_equal, 1.0, 0, 1, [[0, N_HEADS], [-1, NBLK]])
            fill_where(seqmask[:, :], ALU.is_ge, 0.0, 0, 1, [[-N_HEADS, NS]])
            fill_where(gmask3[:, :, :], ALU.is_ge, 0.0, 0, 1, [[-N_HEADS, NS], [-R, N_KV]])
            for g in range(NPG):
                for half in range(2):
                    settle()
                    step(nc.gpsimd.memset(blkpad[half * CMP:(half + 1) * CMP, g, 2 * g + half:2 * g + half + 1], 1.0))
            settle()
            fill_where(headmask[:, :], ALU.is_ge, 0.0, NBLK - 1, -1, [[NBLK, N_HEADS]])
            fill_where(seqmask[:, :], ALU.is_ge, 0.0, N_HEADS - 1, -1, [[N_HEADS, NS]])
            fill_where(gmask3[:, :, :], ALU.is_ge, 0.0, R - 1, -1, [[N_HEADS, NS], [R, N_KV]])
            step(nc.gpsimd.tensor_copy(ident_r[:, :], ident[:, :]))
            step(nc.gpsimd.tensor_copy(causal_r[:, :], tmp[:, 0, 0:P]))
            settle()
            nc.gpsimd.tensor_scalar(offseq[:, :], seqmask[:, :], 1.0, -NEG, ALU.subtract, ALU.mult)\
                .then_inc(consts_ready, 1)
            with pool.Fori(0, C_END // 2) as i:
                for b in range(2):
                    for j in range(2):
                        x = slice(j * CHUNK // 2, (j + 1) * CHUNK // 2)
                        pool.wait_ge(hi_done, 4 * i + 2 * b + j + 1)
                        nc.gpsimd.tensor_tensor(wl[b][:, x], raw[b][:, x], wh[b][:, x].bitcast(F32), ALU.subtract)\
                            .then_inc(lo_done, 1)

        def pair(ap):
            return ap.rearrange("p (a c) -> p a c", a=2)

        @block.scalar
        def _(act):
            def hi(k, b, first=False):
                act.wait_ge(raw_landed[b], 32 * k + 32)
                if not first:
                    act.wait_ge(pe_done, 4 * k + 2 * b - 2)
                for j in range(2):
                    x = slice(j * CHUNK // 2, (j + 1) * CHUNK // 2)
                    nc.scalar.activation(wh[b][:, x], raw[b][:, x], ACT.Copy).then_inc(hi_done, 1)

            def norm(k, ready, between=None):
                for ft in range(KT):
                    ready(ft)
                    if ft >= 2:
                        act.wait_ge(sq_summed, KT * k + ft - 1)
                    nc.scalar.activation(tmp[:, ft % 2, :], xT[:, ft, :], ACT.Square).then_inc(sq_done, 1)
                act.wait_ge(sq_summed, KT * k + KT)
                sums = D[0][:, :, 0:HALF] if k == 2 else E[:, 0:2, 0:HALF]
                nc.scalar.activation(pair(tmp[:, 0, :]), sums, ACT.Sqrt, bias=eps_col[:, 0:1])\
                    .then_inc(rms_done, 1)
                if between:
                    between()
                if k < 2:
                    for ft in range(KT):
                        act.wait_ge(normed, KT * k + ft + 1)
                        nc.scalar.activation(hH[:, ft, :], th[:, ft % 2, :], ACT.Copy).then_inc(norm_hi, 1)

            def table(dst, src):
                act.dma_start(dst, src).then_inc(tables_landed, 16)

            act.dma_start(xs_in[:, :], x_sample[:, 0, :]).then_inc(xs_landed, 16)
            table(vecs[V_WSC:V_WLRU, :], w_sc_conv[0])
            table(vecs[V_WLRU:V_BLRU, :], w_lru_conv[0])
            table(vecs[V_BLRU:V_BGATE, :], b_lru_conv)
            table(vecs[V_BGATE:V_LAM, :], b_lru_gate[0])
            table(vecs[V_LAM:V_SSC, :], lru_lambda)
            table(vecs[V_SSC:V_SLC, :], state_sconv[0].rearrange("s k n -> (s k) n"))
            table(vecs[V_SLC:V_SH, :], state_lru_conv[0].rearrange("s k n -> (s k) n"))
            table(vecs[V_SH:V_ROWS, :], state_lru_h[0])
            for n, g in enumerate((norm1_g[0], norm2_g[0], final_g)):
                table(g_rows[n * KT:(n + 1) * KT, :], g.rearrange("(k p) -> k p", p=P))
            for n, w in enumerate((w_cmp_k, w_cmp_v)):
                for half in range(2):
                    table(wc_rows[:, n, half, :], w[0])
                    table(wc_tok[half * CMP:(half + 1) * CMP, n, :], w[0])
            act.dma_start(pages[:, :], page_table.rearrange("s g -> (s g)").unsqueeze(0)).then_inc(pages_landed, 16)
            act.wait_ge(pool_step, 14)
            for gate in range(2):
                v = w_lru_gate[0, gate].rearrange("(t h) i j -> h i t j", h=2)
                for half in range(2):
                    rows = slice(half * DH, (half + 1) * DH)
                    act.dma_start(wg[rows, gate, :, half * DH:(half + 1) * DH], v[half]).then_inc(wg_landed, 16)
            act.wait_ge(consts_ready, 1)
            norm(0, lambda ft: act.wait_ge(x_evac, 2 * ft + 2), lambda: (hi(0, 0, True), hi(0, 1, True)))
            act.dma_start(win_s[0, :, 0:PAST - 1].rearrange("s t c g d -> t s (c g d)"),
                          cache_win[0, :, 1:PAST].rearrange("s t c g d -> t s (c g d)")).then_inc(rows_moved, 16)
            act.dma_start(sconv_s[0, :, 0, :], state_sconv[0, :, 1, :]).then_inc(rows_moved, 16)
            act.dma_start(lruconv_s[0, :, 0:2, :], state_lru_conv[0, :, 1:3, :]).then_inc(rows_moved, 16)
            act.wait_ge(lam_abs, 1)
            nc.scalar.activation(spl[:, 2, :], spl[:, 1, :], ACT.Exp).then_inc(lam_exp, 1)
            for k in (1, 2, 3):
                for b in range(2):
                    hi(k, b)
            act.wait_ge(hb_ready, 1)
            for g in range(2 * WT):
                act.wait_ge(gate_mm, g + 1)
                dst = (t0 if g < WT else t1)[:, g % WT, :]
                nc.scalar.activation(pair(dst), E[:, 2 * (g % 2):2 * (g % 2) + 2, 0:HALF], ACT.Tanh, scale=0.5,
                                     bias=hb[:, g % WT, g // WT:g // WT + 1]).then_inc(gate_tanh, 1)
            for ft in range(WT):
                act.wait_ge(tile_free[ft % 2], 1 + C_B + ft // 2 + 1)
                nc.scalar.activation(vH[:, ft, :], th[:, ft % 2, :], ACT.Copy).then_inc(v_hi, 1)
                if ft % 2 == 1:
                    hi(4, ft // 2)
            act.wait_ge(neg_la, WT)
            nc.scalar.activation(la[:, :, :], t0[:, :, :], ACT.Exp, scale=-1.0).then_inc(la_exp, 1)
            nc.scalar.activation(lm[:, :, :], t0[:, :, :], ACT.Tanh).then_inc(la_tanh, 1)
            hi(5, 0)
            act.wait_ge(mult_sq, 1)
            nc.scalar.activation(lm[:, :, :], lm[:, :, :], ACT.Sqrt).then_inc(mult_ready, 1)
            hi(5, 1)
            for m in range(2):
                act.wait_ge(tile_free[m], 1 + C_MIX1)
            act.wait_ge(h_ready, WT + 2)
            nc.scalar.activation(la[:, :, :], cb[:, :, :], ACT.Square).then_inc(y_sq, 1)
            act.wait_ge(gelu_arg, 2)
            nc.scalar.activation(la[:, :, :], la[:, :, :], ACT.Tanh, scale=GELU_C).then_inc(gelu_tanh, 1)
            act.wait_ge(lr_prod, 1)
            nc.scalar.activation(lrH[:, :, :], lm[:, :, :], ACT.Copy).then_inc(lr_hi, 1)

            for c0 in (C_MIX1, C_MIX2):
                with act.Fori(0, 4) as i:
                    for m in range(2):
                        act.wait_ge(pe_done, 4 * i + 2 * c0 + m + 1)
                        if m == 1:
                            hi(i + c0 // 2 + 1, 0)
                        nc.scalar.activation(pair(th[:, m, :]), D[m][:, :, 0:HALF], ACT.Tanh, scale=0.5)\
                            .then_inc(tile_free[m], 1)
                    hi(i + c0 // 2 + 1, 1)
            act.wait_ge(tails_evac, 3)
            act.dma_start(wt_raw[:, :, :], w_in[0, :, COL_G:COL_G + P].rearrange("(k p) n -> p k n", p=P))\
                .then_inc(gcols_landed, 16)
            act.wait_ge(gcols_landed, 16)
            nc.scalar.activation(wtH[:, :, :], wt_raw[:, :, :], ACT.Copy).then_inc(wt_hi, 1)
            with act.Fori(0, 2) as i:
                for b in range(2):
                    hi(i + C_Q // 2 + 1, b)
            act.wait_ge(gnsa_mm, 1)
            gT = rstd[0:3 * N_HEADS, :]
            nc.scalar.activation(pair(gT), E[0:3 * N_HEADS, 2:4, 0:HALF], ACT.Tanh, scale=0.5).then_inc(gnsa_tanh, 1)
            with act.Fori(0, 3) as i:
                for b in range(2):
                    hi(i + C_KV // 2 + 1, b)
            for c in range(C_GM0, C_NSA):
                for m in range(2):
                    act.wait_ge(pe_done, 2 * c + m + 1)
                    nc.scalar.activation(pair(th0[:, 2 * (c - C_GM0) + m, :]), D[m][:, :, 0:HALF], ACT.Tanh, scale=0.5)\
                        .then_inc(tile_free[m], 1)
                hi((c + 2) // 2, c % 2)
                if c == C_GM0:
                    act.wait_ge(cmp_shift, 3)
                    nc.scalar.activation(th[:, 0, 0:SEQ], th[:, 0, 0:SEQ], ACT.Exp).then_inc(cmp_exp, 1)
            for n in range(12):
                act.wait_ge(kv_turned, n + 1)
                f = slice((n % 2) * P, (n % 2) * P + P)
                dst = kvc_tok[:, :, n // 2, f] if n < 4 else kv_tok[:, :, n // 2 - 2, f]
                nc.scalar.activation(dst, E[:, (n + 1) % 3, :].rearrange("p (q x) -> p q x", q=QT), ACT.Copy)\
                    .then_inc(kv_evac, 1)
            for q in range(QT):
                act.wait_ge(cmp_out, q + 1)
                nc.scalar.activation(onsa[:, q, :].rearrange("p (a c) -> p a c", a=2), D[q % 2][:, :, :], ACT.Copy)\
                    .then_inc(cmp_evac, 1)
            with act.Fori(0, 4) as it:
                for u in range(32):
                    qi = u % 4
                    act.wait_ge(nmax_done, 32 * it + u + 1)
                    act.wait_ge(probs_turned, 32 * it + u + 1)
                    nc.scalar.activation(prob[u % 4][:, 0:(qi + 1) * P], E[:, u % 4, 0:(qi + 1) * P], ACT.Exp,
                                         bias=anm[:, u % 8:u % 8 + 1],
                                         accum_out=asum[:, (u // 4) % 4, qi:qi + 1]).then_inc(exp_done, 1)
            for y in range(3):
                if y > 0:
                    for s in range(NS):
                        act.wait_ge(s_k_turned, (y - 1) * NS + s + 1)
                        if y == 2 or s >= 2:
                            act.wait_ge(s_k_used, (y - 1) * NS + s - 1)
                        nc.scalar.activation(kTs[s % 2][:, :, :], E[:, s % 2, :].rearrange("p (f t) -> p f t", f=2),
                                             ACT.Copy).then_inc(s_k_evac, 1)
                act.wait_ge(s_nmax, y + 1)
                n = NBLK_S if y == 0 else PAST + NS
                nc.scalar.activation(p_sb[:, 0:n], s_sb[:, 0:n], ACT.Exp, bias=smalls[:, 0, 0:1],
                                     accum_out=smalls[:, 1, 0:1]).then_inc(s_exp, 1)
            for ft in range(KT):
                act.wait_ge(on_turned, ft + 1)
                nc.scalar.activation(onH[:, ft, 0:SEQ], E[:, ft % 4, :], ACT.Copy).then_inc(on_hi, 1)
            for c in range(C_NSA, C_WO):
                for m in range(2):
                    n = 2 * (c - C_NSA) + m
                    act.wait_ge(mix_sum, n + 1)
                    nc.scalar.activation(hH[:, n, :], th[:, m, :], ACT.Copy).then_inc(mix_hi, 1)
                hi((c + 2) // 2, c % 2)
            for c in range(C_WO, C_FI):
                hi((c + 2) // 2, c % 2)
            norm(1, lambda ft: act.wait_ge(tile_free[ft % 2], 1 + C_WO + ft // 2 + 1))
            with act.Fori(0, D_FF // CW) as i:
                for m in range(2):
                    act.wait_ge(pe_done, 4 * i + 2 * C_FI + m + 1)
                    nc.scalar.activation(pair(th[:, m, :]), D[m][:, :, 0:HALF], ACT.Tanh, scale=0.5)\
                        .then_inc(ffn_tanh, 1)
                hi(i + C_FI // 2 + 1, 0)
                for m in range(2):
                    act.wait_ge(tile_free[m], 2 * i + C_FI + 3)
                    nc.scalar.activation(actH[:, bass.ds(2 * i + m, 1), :].squeeze(1), tmp[:, m, :], ACT.Copy)\
                        .then_inc(act_hi, 1)
                hi(i + C_FI // 2 + 1, 1)
            for c in range(C_FO, C_END - 2):
                hi((c + 2) // 2, c % 2)
            norm(2, lambda ft: act.wait_ge(x_last, 4 + ft + 1))
            for q in range(QT):
                act.wait_ge(y_turned, q + 1)
                nc.scalar.activation(y_tok[q][:, 0:512], D[q % 2][:, 0, :], ACT.Copy).then_inc(y_evac_a, 1)

        @block.vector
        def _(dve):
            steps = [0]

            def step(ins):
                ins.then_inc(vec_step, 1)
                steps[0] += 1

            def settle():
                dve.wait_ge(vec_step, steps[0])

            def tile(c, m):
                dve.wait_ge(pe_done, 2 * c + m + 1)
                return D[m][:, :, 0:HALF]

            def norm(k):
                dve.wait_ge(rms_done, k + 1)
                if k > 0:
                    dve.wait_ge(normed, KT * k)
                nc.vector.reciprocal(rstd[:, :], tmp[:, 0, :]).then_inc(rstd_done, 1)
                dve.wait_ge(rstd_done, k + 1)
                for ft in range(KT + 1):
                    if ft < KT:
                        if k == 2:
                            nc.vector.scalar_tensor_tensor(yT[:, ft, :], xT[:, ft, :], g_cols[:, k, ft:ft + 1],
                                                           rstd[:, :], ALU.mult, ALU.mult).then_inc(y_ready, 1)
                            continue
                        if ft >= 2:
                            dve.wait_ge(norm_lo, KT * k + ft - 1)
                        nc.vector.scalar_tensor_tensor(th[:, ft % 2, :], xT[:, ft, :], g_cols[:, k, ft:ft + 1],
                                                       rstd[:, :], ALU.mult, ALU.mult).then_inc(normed, 1)
                    if ft > 0 and k < 2:
                        dve.wait_ge(norm_hi, KT * k + ft)
                        nc.vector.tensor_tensor(hL[:, ft - 1, :], th[:, (ft - 1) % 2, :],
                                                hH[:, ft - 1, :].bitcast(F32), ALU.subtract).then_inc(norm_lo, 1)

            for ft in range(KT):
                dve.wait_ge(x_turned, ft + 1)
                e = 2 * (ft % 2)
                nc.vector.tensor_copy(xT[:, ft, 0:SEQ], E[:, e, :]).then_inc(x_evac, 1)
                nc.vector.tensor_copy(xT[:, ft, SEQ:T], E[:, e + 1, 0:NS]).then_inc(x_evac, 1)
            dve.wait_ge(tables_turned, 1)
            v = D[1][:, 0, 0:WT * 64].rearrange("p (t r) -> p t r", t=WT)
            nc.vector.tensor_copy(vecT[:, :, :], v[:, :, 0:V_ROWS]).then_inc(tables_evac, 1)
            nc.vector.tensor_copy(g_cols[:, :, :], D[1][:, 1, 0:3 * KT].rearrange("p (n k) -> p n k", n=3))\
                .then_inc(tables_evac, 1)
            nc.vector.tensor_copy(wcT[:, :, :], D[1][:, 1, 64:64 + 2 * CMP].rearrange("p (n j) -> p n j", n=2))\
                .then_inc(tables_evac, 1)
            dve.wait_ge(tables_evac, 3)
            nc.vector.tensor_scalar(hb[:, :, :], vecT[:, :, V_BGATE:V_LAM], 0.5, None, ALU.mult).then_inc(hb_ready, 1)
            lam = vecT[:, :, V_LAM:V_LAM + 1].squeeze(2)
            step(nc.vector.tensor_scalar(spl[:, 0, :], lam, -1.0, None, ALU.mult))
            settle()
            step(nc.vector.tensor_scalar(spl[:, 3, :], spl[:, 0, :], 0.0, 4.0, ALU.max, ALU.mult))
            nc.vector.tensor_tensor(spl[:, 1, :], spl[:, 0, :], lam, ALU.min).then_inc(lam_abs, 1)
            norm(0)
            dve.wait_ge(lam_exp, 1)
            step(nc.vector.tensor_scalar(spl[:, 4, :], spl[:, 2, :], 2.0, None, ALU.add))
            settle()
            step(nc.vector.reciprocal(spl[:, 5, :], spl[:, 4, :]))
            settle()
            step(nc.vector.tensor_tensor(spl[:, 6, :], spl[:, 2, :], spl[:, 5, :], ALU.mult))
            settle()
            step(nc.vector.tensor_tensor(spl[:, 7, :], spl[:, 6, :], spl[:, 6, :], ALU.mult))
            settle()
            step(nc.vector.tensor_scalar(spl[:, 8, :], spl[:, 7, :], 1.0 / 15, None, ALU.mult))
            for q in (13, 11, 9, 7, 5, 3):
                settle()
                step(nc.vector.scalar_tensor_tensor(spl[:, 8, :], spl[:, 8, :], 1.0 / q, spl[:, 7, :],
                                                    ALU.add, ALU.mult))
            settle()
            step(nc.vector.scalar_tensor_tensor(spl[:, 9, :], spl[:, 8, :], 1.0, spl[:, 6, :], ALU.add, ALU.mult))
            settle()
            step(nc.vector.scalar_tensor_tensor(spl[:, 10, :], spl[:, 9, :], 8.0, spl[:, 3, :], ALU.mult, ALU.add))
            settle()
            sp4 = spl[:, 10, :]

            def conv(ft, dst, ext, w0, taps, state, done, bias=None):
                w = [vecT[:, ft, w0 + k:w0 + k + 1] for k in range(taps)]
                new = ext[:, ft, taps - 1 + SEQ:taps - 1 + T]
                old = vecT[:, ft, state:state + NS * (taps - 1)].rearrange("p (s k) -> p k s", k=taps - 1)
                cols = [(dst[:, ft, 0:SEQ], [ext[:, ft, k:k + SEQ] for k in range(taps)]),
                        (dst[:, ft, SEQ:T], [old[:, k, :] for k in range(taps - 1)] + [new])]
                for k in range(taps):
                    for d, src in cols:
                        if k == 0 and bias is not None:
                            step(nc.vector.tensor_scalar(d, src[0], w[0], bias, ALU.mult, ALU.add))
                        elif k == 0:
                            step(nc.vector.tensor_scalar(d, src[0], w[0], None, ALU.mult))
                        elif k < taps - 1:
                            step(nc.vector.scalar_tensor_tensor(d, src[k], w[k], d, ALU.mult, ALU.add))
                        else:
                            nc.vector.scalar_tensor_tensor(d, src[k], w[k], d, ALU.mult, ALU.add).then_inc(done, 1)
                    if k < taps - 1:
                        settle()

            dve.wait_ge(consts_ready, 1)
            for n in range(WT):
                c, m = C_XL + n // 2, n % 2
                nc.vector.tensor_copy(pair(exl[:, n, 3:3 + T]), tile(c, m)).then_inc(tile_free[m], 1)
            for n in range(WT):
                c, m = C_C + n // 2, n % 2
                dve.wait_ge(tile_free[n % 2], 1 + n // 2 + 1)
                conv(n, xc, exl, V_WLRU, 4, V_SLC, xc_ready, vecT[:, n, V_BLRU:V_BLRU + 1])
                nc.vector.tensor_copy(pair(cb[:, n, :]), tile(c, m)).then_inc(tile_free[m], 1)
            for n in range(WT):
                c, m = C_X + n // 2, n % 2
                dve.wait_ge(tile_free[m], 1 + C_C + n // 2 + 1)
                nc.vector.tensor_tensor(pair(eu[:, n, 2:2 + T]), tile(c, m), pair(cb[:, n, :]), ALU.mult)\
                    .then_inc(tile_free[m], 1)
                dve.wait_ge(tile_free[m], 1 + C_X + n // 2 + 1)
                conv(n, cb, eu, V_WSC, 3, V_SSC, cx_ready)
            for n in range(WT + 1):
                if n < WT:
                    c, m = C_B + n // 2, n % 2
                    dve.wait_ge(cx_ready, 2 * n + 2)
                    if n >= 2:
                        dve.wait_ge(v_lo, n - 1)
                    nc.vector.tensor_tensor(pair(th[:, m, :]), tile(c, m), pair(cb[:, n, :]), ALU.mult)\
                        .then_inc(tile_free[m], 1)
                if n > 0:
                    dve.wait_ge(v_hi, n)
                    nc.vector.tensor_tensor(vL[:, n - 1, :], th[:, (n - 1) % 2, :], vH[:, n - 1, :].bitcast(F32),
                                            ALU.subtract).then_inc(v_lo, 1)

            def y_tile(n):
                c, m = C_YL + n // 2, n % 2
                if n == 0:
                    for k in range(2):
                        dve.wait_ge(tile_free[k], 1 + C_YL)
                nc.vector.tensor_copy(pair(cb[:, n, :]), tile(c, m)).then_inc(tile_free[m], 1)

            dve.wait_ge(gate_tanh, WT)
            for ft in range(WT):
                nc.vector.tensor_scalar(t0[:, ft, :], t0[:, ft, :], 1.0, sp4[:, ft:ft + 1], ALU.add, ALU.mult)\
                    .then_inc(neg_la, 1)
            y_tile(0)
            dve.wait_ge(la_exp, 1)
            dve.wait_ge(la_tanh, 1)
            step(nc.vector.tensor_tensor(t0[:, :, :], la[:, :, :], la[:, :, :], ALU.mult))
            settle()
            nc.vector.scalar_tensor_tensor(lm[:, :, :], t0[:, :, :], 1.0, lm[:, :, :], ALU.add, ALU.mult)\
                .then_inc(mult_sq, 1)
            y_tile(1)
            dve.wait_ge(gate_tanh, 2 * WT)
            step(nc.vector.scalar_tensor_tensor(t1[:, :, :], t1[:, :, :], 1.0, xc[:, :, :], ALU.add, ALU.mult))
            dve.wait_ge(mult_ready, 1)
            step(nc.vector.memset(lm[:, :, 0:1], 1.0))
            step(nc.vector.memset(la[:, :, 0:1], 0.0))
            settle()
            y_tile(2)
            step(nc.vector.scalar_tensor_tensor(t1[:, :, :], lm[:, :, :], 0.5, t1[:, :, :], ALU.mult, ALU.mult))
            y_tile(3)
            settle()
            dve.wait_ge(mult_sq, 1)
            for ft in range(WT):
                nc.vector.tensor_tensor_scan(t0[:, ft, 0:SEQ], la[:, ft, 0:SEQ], t1[:, ft, 0:SEQ], 0.0,
                                             ALU.mult, ALU.add).then_inc(h_ready, 1)
            nc.vector.tensor_tensor(t0[:, :, SEQ:T], la[:, :, SEQ:T], vecT[:, :, V_SH:V_ROWS], ALU.mult)\
                .then_inc(h_ready, 1)
            dve.wait_ge(h_ready, WT + 1)
            nc.vector.tensor_tensor(t0[:, :, SEQ:T], t0[:, :, SEQ:T], t1[:, :, SEQ:T], ALU.add).then_inc(h_ready, 1)
            dve.wait_ge(tails_turned, 1)
            nc.vector.tensor_copy(st_u[:, :], E[0:2 + NS, 0, :]).then_inc(tails_evac, 1)
            nc.vector.tensor_copy(st_x[:, :], E[0:3 + NS, 1, :]).then_inc(tails_evac, 1)
            dve.wait_ge(y_sq, 1)
            nc.vector.tensor_scalar(la[:, :, :], la[:, :, :], 0.044715, 1.0, ALU.mult, ALU.add).then_inc(gelu_arg, 1)
            dve.wait_ge(gelu_arg, 1)
            nc.vector.tensor_tensor(la[:, :, :], la[:, :, :], cb[:, :, :], ALU.mult).then_inc(gelu_arg, 1)
            dve.wait_ge(gelu_tanh, 1)
            step(nc.vector.scalar_tensor_tensor(la[:, :, :], la[:, :, :], 1.0, cb[:, :, :], ALU.add, ALU.mult))
            settle()
            dve.wait_ge(h_ready, WT + 2)
            nc.vector.scalar_tensor_tensor(lm[:, :, :], la[:, :, :], 0.5, t0[:, :, :], ALU.mult, ALU.mult)\
                .then_inc(lr_prod, 1)
            dve.wait_ge(lr_hi, 1)
            nc.vector.tensor_tensor(lrL[:, :, :], lm[:, :, :], lrH[:, :, :].bitcast(F32), ALU.subtract)\
                .then_inc(lr_lo, 1)

            dve.wait_ge(tails_evac, 2)
            with dve.Fori(0, 4) as i:
                for m in range(2):
                    dve.wait_ge(pe_done, 4 * i + 2 * C_MIX1 + 2 + m + 1)
                    nc.vector.scalar_tensor_tensor(pair(acc[:, bass.ds(2 * i + m, 1), :].squeeze(1)),
                                                   pair(th[:, m, :]), 1.0, D[m][:, :, 0:HALF], ALU.add, ALU.mult)\
                        .then_inc(tile_free[m], 1)
            dve.wait_ge(tails_turned, 2)
            nc.vector.tensor_copy(st_h[:, :], E[0:1 + NS, 2, :]).then_inc(tails_evac, 1)
            with dve.Fori(0, 4) as i:
                for m in range(2):
                    dve.wait_ge(pe_done, 4 * i + 2 * C_MIX2 + 2 + m + 1)
                    dve.wait_ge(mixed, 2 * i + m + 1)
                    nc.vector.scalar_tensor_tensor(pair(tmp[:, m, :]), pair(th[:, m, :]), 1.0, D[m][:, :, 0:HALF],
                                                   ALU.add, ALU.mult).then_inc(tile_free[m], 1)
                    dve.wait_ge(tile_free[m], 2 * i + C_MIX2 + 1 + 2)
                    a = acc[:, bass.ds(2 * i + m, 1), :].squeeze(1)
                    nc.vector.tensor_tensor(a, a, tmp[:, m, :], ALU.add).then_inc(mixed, 1)
            dve.wait_ge(wt_hi, 1)
            nc.vector.tensor_tensor(wtL[:, :, :], wt_raw[:, :, :], wtH[:, :, :].bitcast(F32), ALU.subtract)\
                .then_inc(wt_lo, 1)
            with dve.Fori(0, 2) as i:
                for b in range(2):
                    for m in range(2):
                        dve.wait_ge(pe_done, 4 * i + 2 * (C_Q + b) + m + 1)
                        rows = slice(b * DH, (b + 1) * DH)
                        nc.vector.tensor_scalar(pair(qT[rows, bass.ds(4 * i + 2 * m, 1), :].squeeze(1)),
                                                D[m][0:DH, :, 0:HALF], SCALE, None, ALU.mult).then_inc(q_even, 1)
                        dve.wait_ge(q_even, 4 * i + 2 * b + m + 1)
                        nc.vector.tensor_scalar(pair(qT[rows, bass.ds(4 * i + 2 * m + 1, 1), :].squeeze(1)),
                                                D[m][DH:P, :, 0:HALF], SCALE, None, ALU.mult).then_inc(tile_free[m], 1)
            places = [(vT, 0), (vT, 2), (kT, 0), (vT, 4), (kT, 2), (vT, 6)]
            for n in range(12):
                c, m = C_KV + n // 2, n % 2
                buf, o = places[n // 2]
                nc.vector.tensor_copy(pair(buf[:, o + m, :]), tile(c, m)).then_inc(tile_free[m], 1)
                if 4 <= n < 8:
                    t = n - 4
                    dve.wait_ge(tile_free[t % 2], 1 + C_KV + t // 2 + 1)
                    settle()
                    prodv = tmp[:, 0, 0:SEQ].rearrange("p (k j) -> p k j", j=CMP)
                    step(nc.vector.tensor_tensor(prodv, vT[:, t, 0:SEQ].rearrange("p (k j) -> p k j", j=CMP),
                                                 wcT[:, t // 2, :].unsqueeze(1).to_broadcast([P, NBLK, CMP]), ALU.mult))
                    settle()
                    step(nc.vector.reduce_sum(kc_sum[:, t, :], prodv, AX.X))
            dve.wait_ge(gnsa_turned, 1)
            nc.vector.tensor_scalar(gates_tok[:, :, :], E[:, 0, 0:QT * 48].rearrange("p (q c) -> p q c", q=QT),
                                    1.0, 0.5, ALU.add, ALU.mult).then_inc(gates_ready, 1)
            nc.vector.tensor_scalar(gates_stok[:, :], E[0:NS, 1, 0:48], 1.0, 0.5, ALU.add, ALU.mult)\
                .then_inc(gates_ready, 1)
            settle()
            for j in range(2):
                rows = slice(j * DH, (j + 1) * DH)
                nc.vector.tensor_copy(kc_blk[rows, :, j * NBLK:(j + 1) * NBLK], kc_sum[rows, 0:2, :])\
                    .then_inc(cmp_sums, 1)
            dve.wait_ge(vc_turned, 1)
            vc_tok = tmp[0:NBLK, 1, 0:KVC]
            nc.vector.tensor_copy(vc_tok, E[0:NBLK, 2, 0:KVC]).then_inc(vc_evac, 1)
            dve.wait_ge(cmp_scores, 1)
            full = [P, QT, N_HEADS, NBLK]
            cs = th[:, 0, 0:SEQ].rearrange("p (q h k) -> p q h k", q=QT, k=NBLK)
            cs3 = th[:, 0, 0:SEQ].rearrange("p (n k) -> p n k", k=NBLK)
            pc = th[:, 1, 0:SEQ]
            cols3 = [P, QT * N_HEADS, NBLK]
            cmx, csum, crc = smalls[:, 0, :], smalls[:, 1, :], smalls[:, 2, :]
            nc.vector.tensor_tensor(cs, E[:, 0, :].rearrange("p (q h k) -> p q h k", q=QT, k=NBLK),
                                    cmask[:, :, :, :].to_broadcast(full), ALU.add).then_inc(cmp_shift, 1)
            dve.wait_ge(cmp_shift, 1)
            nc.vector.reduce_max(cmx, cs3, AX.X).then_inc(cmp_shift, 1)
            dve.wait_ge(cmp_shift, 2)
            nc.vector.tensor_tensor(cs3, cs3, cmx.unsqueeze(2).to_broadcast(cols3), ALU.subtract).then_inc(cmp_shift, 1)
            dve.wait_ge(cmp_exp, 1)
            step(nc.vector.tensor_tensor(cs, cs, cmask01[:, :, :, :].to_broadcast(full), ALU.mult))
            settle()
            step(nc.vector.reduce_sum(csum, cs3, AX.X))
            settle()
            step(nc.vector.tensor_scalar(csum, csum, TINY, None, ALU.max))
            settle()
            step(nc.vector.reciprocal(crc, csum))
            settle()
            gt = gates_tok[:, :, :].rearrange("p q (h c) -> p q h c", c=3)
            step(nc.vector.tensor_tensor(crc.rearrange("p (q h) -> p q h", q=QT),
                                         crc.rearrange("p (q h) -> p q h", q=QT), gt[:, :, :, 0], ALU.mult))
            settle()
            nc.vector.tensor_tensor(pc.rearrange("p (n k) -> p n k", k=NBLK), cs3,
                                    crc.unsqueeze(2).to_broadcast(cols3), ALU.mult).then_inc(cmp_prob, 1)
            dve.wait_ge(vc_rep, 1)
            dve.wait_ge(pe_done, 2 * C_NSA)
            full = [P, N_KV, R, DH]
            nc.vector.tensor_tensor(vbig[:, :].rearrange("p (g r d) -> p g r d", g=N_KV, r=R),
                                    E[:, 3, 0:KVC].rearrange("p (g d) -> p g d", g=N_KV).unsqueeze(2).to_broadcast(full),
                                    headmask[:, :].rearrange("p (g r) -> p g r", g=N_KV).unsqueeze(3).to_broadcast(full),
                                    ALU.mult).then_inc(vbig_ready, 1)
            dve.wait_ge(pc_turned, 1)
            nc.vector.tensor_copy(pcT[:, :, :], E[:, 0, :].rearrange("p (q x) -> p q x", q=QT)).then_inc(pc_evac, 1)
            def stage(f, rp, n):
                if n < 2:
                    src, dst = qT[:, bass.ds(4 * f + 2 * rp + n, 1), 0:SEQ], q_st[rp][n]
                else:
                    src, dst = kT[:, bass.ds(f + 2 * (n - 2), 1), 0:SEQ], k_st[rp][n - 2]
                nc.vector.tensor_copy(dst, src.squeeze(1)).then_inc(staged, 1)

            for n in range(4):
                stage(0, 0, n)
            for g in range(3):
                dve.wait_ge(kv_turned, 4 * (g + 1))
                dst = kvcs_tok[:, :, :] if g == 0 else kvs_tok[:, 2 * g - 2:2 * g, :]
                nc.vector.tensor_copy(dst, E[0:NS, 3, :].rearrange("p (c x) -> p c x", c=2)).then_inc(kvs_evac, 1)

            dve.wait_ge(cmp_evac, QT)
            with dve.Fori(0, 2) as f:
                for u in range(64 + 5):
                    if u < 64:
                        dve.wait_ge(scores_done, 64 * f + u + 2)
                        nc.vector.reduce_max(anm[:, u % 8:u % 8 + 1], E[:, u % 4, 0:(u % 4 + 1) * P], AX.X,
                                             negate=True).then_inc(nmax_done, 1)
                    if 2 <= u < 66:
                        w = u - 2
                        dve.wait_ge(probs_turned, 64 * f + w + 1 + 4)
                        dve.wait_ge(pv_done, 64 * f + w + 1)
                        n = w % 4 + 1
                        nc.vector.tensor_copy(probT[w % 2][:, 0:n, :],
                                              D[0][:, w % 2, 0:n * P].rearrange("p (k x) -> p k x", k=n))\
                            .then_inc(probT_done, 1)
                    if u in (8, 12, 16, 20):
                        stage(f, 1, (u - 8) // 4)
                    if u in (36, 40, 44, 48):
                        stage(1 - f, 0, (u - 36) // 4)
                    g = (u - 5) // 4
                    s0 = 64 * f + 4 * g
                    if u >= 5 and u % 4 == 1 and g < 16:
                        nc.vector.tensor_scalar(acf[:, 0, :], asum[:, g % 4, :], TINY, None, ALU.max)\
                            .then_inc(att_step, 1)
                    if u >= 5 and u % 4 == 2:
                        dve.wait_ge(att_step, s0 + 1)
                        nc.vector.reciprocal(acf[:, 1, :], acf[:, 0, :]).then_inc(att_step, 1)
                    h = 8 * f + 2 * (g // 8) + (g // 4) % 2 + 4 * ((g // 2) % 2)
                    a = g % 2
                    o4 = tmp[:, 0, 0:QT * DH].rearrange("p (q d) -> p q d", q=QT)
                    if u >= 5 and u % 4 == 3:
                        dve.wait_ge(att_step, s0 + 2)
                        nc.vector.tensor_tensor(acf[:, 0, :], acf[:, 1, :],
                                                gates_tok[:, :, bass.ds(3 * h + 1 + a, 1)].squeeze(2), ALU.mult)\
                            .then_inc(att_step, 1)
                        dve.wait_ge(att_step, s0 + 3)
                        dve.wait_ge(pv_done, 64 * f + 4 * g + 4 + 2)
                        nc.vector.tensor_tensor(o4, D[1][:, g % 2, 0:QT * DH].rearrange("p (q d) -> p q d", q=QT),
                                                acf[:, 0, :].unsqueeze(2).to_broadcast([P, QT, DH]), ALU.mult)\
                            .then_inc(o_added, 1)
                    if u >= 8 and u % 4 == 0:
                        dve.wait_ge(o_added, 16 * f + g + 1 + 2)
                        dst = onsa[:, :, bass.ds(h * DH, DH)]
                        nc.vector.tensor_tensor(dst, dst, o4, ALU.add).then_inc(att_step, 1)
                dve.wait_ge(att_step, 64 * f + 64)

            dve.wait_ge(pv_done, 128 + 2)
            dve.wait_ge(out_written, 16 * STATE_OUTS)
            step(nc.vector.reduce_sum(gmask[:, :], gmask3[:, :, :].rearrange("p s g -> p g s"), AX.X))
            step(nc.vector.memset(q_padf[:, :], 0.0))
            step(nc.vector.memset(q_all[:, :, :], 0.0))
            step(nc.vector.memset(pT_padf[:, :], 0.0))
            step(nc.vector.memset(pT_cmpf[:, :], 0.0))
            settle()
            for f in range(2):
                for j in range(2):
                    rows = slice(j * DH, (j + 1) * DH)
                    src = qT[rows, 4 * f:4 * f + 4, SEQ:T].rearrange("p r s -> p s r")
                    o = f * (P + 2 * R) + j * R
                    diag = q_padf[rows, o:o + NS * QSTEP].rearrange("p (s x) -> p s x", x=QSTEP)[:, :, 0:R]
                    nc.vector.tensor_copy(diag, src).then_inc(qpad_ready, 1)
                    h0 = f * 2 * R + j * R
                    nc.vector.tensor_copy(q_all[rows, f, :].rearrange("p (s h) -> p s h", s=NS)[:, :, h0:h0 + R], src)\
                        .then_inc(qpad_ready, 1)
            dve.wait_ge(qpad_ready, 8)
            for v in range(2):
                for s in range(NS + v):
                    if s < NS:
                        dve.wait_ge(slot_landed[s], 32 * (v + 1))
                        if v == 0 and s >= 2:
                            dve.wait_ge(s_kc_mm, s - 1)
                        elif v == 1:
                            if s < 2:
                                dve.wait_ge(s_kc_mm, NS - 1 + s)
                            else:
                                dve.wait_ge(s_vc_mm, s - 1)
                        shape = [P, NPG * N_KV, DH]
                        nc.vector.tensor_tensor(prod[s % 2][:, :, :, :].rearrange("p a g d -> p (a g) d"),
                                                slot[s][:, :, :].rearrange("p a (g d) -> p (a g) d", g=N_KV),
                                                wc_tok[:, v, :].unsqueeze(1).to_broadcast(shape), ALU.mult)\
                            .then_inc(s_prod, 1)
                    if v == 1 and s > 0:
                        dve.wait_ge(s_vc_mm, s)
                        nc.vector.tensor_copy(vcs[:, s - 1, :], E[0:NBLK_S, 1 + (s - 1) % 2, 0:KVC])\
                            .then_inc(s_vc_evac, 1)
                if v == 0:
                    dve.wait_ge(s_kc_mm, NS)
                    nc.vector.tensor_copy(kcs[:, :, :, :], E[:, 0, 0:NS * 2 * NBLK_S]
                                          .rearrange("p (s f k) -> p s f k", s=NS, f=2)).then_inc(s_kc_evac, 1)
            dve.wait_ge(gates_s_landed, 16 * NS)
            pT_count = 0
            for y in range(3):
                dve.wait_ge(s_scores, y + 1)
                if y == 0:
                    step(nc.vector.tensor_copy(s_sb[:, 0:NBLK_S], E[:, 3, 0:NBLK_S]))
                else:
                    step(nc.vector.tensor_copy(s_sb[:, 0:PAST], E[:, 2, 0:PAST]))
                    step(nc.vector.tensor_tensor(s_sb[:, PAST:PAST + NS], E[:, 3, 0:NS], offseq[:, :], ALU.add))
                settle()
                n = NBLK_S if y == 0 else PAST + NS
                nc.vector.reduce_max(smalls[:, 0, 0:1], s_sb[:, 0:n], AX.X, negate=True).then_inc(s_nmax, 1)
                dve.wait_ge(s_exp, y + 1)
                step(nc.vector.tensor_scalar(smalls[:, 2, 0:1], smalls[:, 1, 0:1], TINY, None, ALU.max))
                settle()
                step(nc.vector.reciprocal(smalls[:, 3, 0:1], smalls[:, 2, 0:1]))
                settle()
                step(nc.vector.tensor_tensor(smalls[:, 2, 0:1], smalls[:, 3, 0:1], gates_s[:, y:y + 1], ALU.mult))
                dve.wait_ge(s_p_turned, y + 1)
                if y == 0:
                    diag = pT_cmpf[:, 0:NS * PSTEP].rearrange("p (s x) -> p s x", x=PSTEP)[:, :, 0:N_HEADS]
                    nc.vector.tensor_copy(diag, D[0][0:NBLK_S, 0, 0:P].rearrange("p (s h) -> p s h", s=NS))\
                        .then_inc(s_pT, 1)
                else:
                    if y == 2:
                        dve.wait_ge(s_out, 2)
                    for g in range(NPG):
                        o = g * NS * P
                        diag = pT_padf[:, o:o + NS * PSTEP].rearrange("p (s x) -> p s x", x=PSTEP)[:, :, 0:N_HEADS]
                        nc.vector.tensor_copy(diag, D[0][:, 0, g * P:(g + 1) * P].rearrange("p (s h) -> p s h", s=NS))\
                            .then_inc(s_pT, 1)
                    nc.vector.tensor_copy(pT_new[:, :], D[0][0:NS, 1, 0:P]).then_inc(s_pT, 1)
                dve.wait_ge(s_out, y + 1)
                nc.vector.tensor_tensor(o_all, D[1][:, 0, 0:KVC].rearrange("p (g d) -> p g d", g=N_KV),
                                        gmask[:, :].unsqueeze(2).to_broadcast([P, N_KV, DH]), ALU.mult)\
                    .then_inc(s_sel, 1)
                dve.wait_ge(s_sel, y + 1)
                step(nc.vector.reduce_sum(o_sel, o_all.rearrange("p g d -> p d g"), AX.X))
                settle()
                if y == 0:
                    step(nc.vector.tensor_scalar(o_sum[:, 0:DH], o_sel, smalls[:, 2, 0:1], None, ALU.mult))
                else:
                    step(nc.vector.scalar_tensor_tensor(o_sum[:, 0:DH], o_sel, smalls[:, 2, 0:1], o_sum[:, 0:DH],
                                                        ALU.mult, ALU.add))
                settle()
            nc.vector.tensor_copy(o_sum[:, DH:2 * DH], o_sum[:, 0:DH]).then_inc(s_sel, 1)
            dve.wait_ge(os_turned, 1)
            for j in range(2):
                rows = slice(j * DH, (j + 1) * DH)
                src = D[1][rows, 1, 0:P].rearrange("p (s f j) -> p j f s", s=NS, j=2)[:, j, :, :]
                nc.vector.tensor_copy(onH[rows, :, SEQ:T], src).then_inc(ons_hi, 1)
                dve.wait_ge(ons_hi, j + 1)
                nc.vector.tensor_tensor(onL[rows, :, SEQ:T], src, onH[rows, :, SEQ:T].bitcast(F32), ALU.subtract)\
                    .then_inc(ons_lo, 1)
            for ft in range(KT):
                dve.wait_ge(on_hi, ft + 1)
                nc.vector.tensor_tensor(onL[:, ft, 0:SEQ], E[:, ft % 4, :], onH[:, ft, 0:SEQ].bitcast(F32),
                                        ALU.subtract).then_inc(on_lo, 1)

            for n in range(KT + 1):
                if n < KT:
                    c, m = C_NSA + n // 2, n % 2
                    if n >= 2:
                        dve.wait_ge(mix_lo, n - 1)
                    nc.vector.scalar_tensor_tensor(pair(tmp[:, m, :]), pair(th0[:, n, :]), 1.0, tile(c, m),
                                                   ALU.add, ALU.mult).then_inc(tile_free[m], 1)
                    dve.wait_ge(tile_free[m], 1 + c + 1)
                    nc.vector.tensor_tensor(th[:, m, :], acc[:, n, :], tmp[:, m, :], ALU.add).then_inc(mix_sum, 1)
                if n > 0:
                    dve.wait_ge(mix_hi, n)
                    nc.vector.tensor_tensor(hL[:, n - 1, :], th[:, (n - 1) % 2, :], hH[:, n - 1, :].bitcast(F32),
                                            ALU.subtract).then_inc(mix_lo, 1)
            with dve.Fori(0, 2) as i:
                for b in range(2):
                    for m in range(2):
                        dve.wait_ge(pe_done, 4 * i + 2 * (C_WO + b) + m + 1)
                        x = pair(xT[:, bass.ds(4 * i + 2 * b + m, 1), :].squeeze(1))
                        nc.vector.scalar_tensor_tensor(x, D[m][:, :, 0:HALF], 0.5, x, ALU.mult, ALU.add)\
                            .then_inc(tile_free[m], 1)
            norm(1)
            with dve.Fori(0, D_FF // CW) as i:
                for m in range(2):
                    dve.wait_ge(ffn_tanh, 2 * i + m + 1)
                    nc.vector.scalar_tensor_tensor(pair(th[:, m, :]), pair(th[:, m, :]), 1.0, D[m][:, :, 0:HALF],
                                                   ALU.add, ALU.mult).then_inc(tile_free[m], 1)
                for m in range(2):
                    dve.wait_ge(pe_done, 4 * i + 2 * C_FI + 2 + m + 1)
                    dve.wait_ge(tile_free[m], 2 * i + C_FI + 2)
                    dve.wait_ge(act_lo, 2 * i + m + 1)
                    nc.vector.tensor_tensor(pair(tmp[:, m, :]), D[m][:, :, 0:HALF], pair(th[:, m, :]), ALU.mult)\
                        .then_inc(tile_free[m], 1)
                for m in range(2):
                    dve.wait_ge(act_hi, 2 * i + m + 1)
                    n = bass.ds(2 * i + m, 1)
                    nc.vector.tensor_tensor(actL[:, n, :].squeeze(1), tmp[:, m, :],
                                            actH[:, n, :].squeeze(1).bitcast(F32), ALU.subtract).then_inc(act_lo, 1)
            for n in range(KT):
                pairs, m = n // 2, n % 2
                dve.wait_ge(pe_done, 2 * (C_FO + 3 * pairs + 2) + m + 1)
                src = D[m][:, :, 0:HALF] if pairs % 2 == 0 else E[:, 2 * m:2 * m + 2, 0:HALF]
                nc.vector.scalar_tensor_tensor(pair(xT[:, n, :]), src, 0.5, pair(xT[:, n, :]), ALU.mult, ALU.add)\
                    .then_inc(x_last, 1)
            norm(2)
            for q in range(QT):
                dve.wait_ge(y_turned, q + 1)
                nc.vector.tensor_copy(y_tok[q][:, 512:1024], D[q % 2][:, 1, :]).then_inc(y_evac_v, 1)
            dve.wait_ge(y_turned, QT + 1)
            for k in range(2):
                nc.vector.tensor_copy(ys_tok[:, k * 512:(k + 1) * 512], E[0:NS, k, :]).then_inc(y_evac_v, 1)

        @block.tensor
        def _(pe):
            mm, turn = nc.tensor.matmul, nc.tensor.transpose

            def product(out2, lhsT, rhs, first, last):
                for a in range(2):
                    ins = mm(out2[:, a, 0:HALF], lhsT, rhs[:, a * HALF:(a + 1) * HALF], start=first, stop=last)
                return ins

            def dense(c, b, nk, xH, xL, x0=0, outs=None, first=True, last=True,
                      ready=None):
                for m in range(2):
                    if outs is None:
                        pe.wait_ge(tile_free[m], c + 1)
                        o = D[m]
                    else:
                        o = outs[m]
                    for k in range(nk):
                        if m == 0 and k in (0, KT // 2):
                            pe.wait_ge(lo_done, 2 * c + (2 if k or nk <= KT // 2 else 1))
                        if ready and m == 0:
                            ready(k)
                        def w(buf):
                            return buf[b][:, k * CW + m * P:k * CW + (m + 1) * P]
                        product(o, w(wh), xH[:, x0 + k, :], first and k == 0, False)
                        product(o, w(wh), xL[:, x0 + k, :], False, False)
                        ins = product(o, w(wl), xH[:, x0 + k, :], False, last and k == nk - 1)
                    ins.then_inc(pe_done, 1)

            def norm_sums(k):
                if k == 2:
                    pe.wait_ge(x_last, 4 + 5)
                for ft in range(KT):
                    pe.wait_ge(sq_done, KT * k + ft + 1)
                    product(D[0] if k == 2 else E[:, 0:2, :], ones[:, :], tmp[:, ft % 2, :], ft == 0, ft == KT - 1).then_inc(sq_summed, 1)

            for m in range(2):
                pe.sem_inc(tile_free[m], 1)
            pe.sem_inc(scores_done, 1)
            pe.sem_inc(mixed, 2)
            pe.sem_inc(exp_done, 4)
            pe.sem_inc(probs_turned, 4)
            pe.sem_inc(probT_done, 2)
            pe.sem_inc(pv_done, 2)
            pe.sem_inc(o_added, 2)
            pe.sem_inc(act_lo, 2)
            pe.sem_inc(x_last, 4)

            pe.wait_ge(consts_ready, 1)
            pe.wait_ge(xs_landed, 16)
            for ft in range(KT):
                if ft >= 2:
                    pe.wait_ge(x_evac, 2 * (ft - 1))
                e = 2 * (ft % 2)
                for q in range(QT):
                    if ft == 0:
                        pe.wait_ge(x_landed[q], 16)
                    turn(E[:, e, q * P:(q + 1) * P], x_in[:, q, ft * P:(ft + 1) * P], ident[:, :])
                turn(E[:, e + 1, 0:NS], xs_in[:, ft * P:(ft + 1) * P], ident[0:NS, 0:NS]).then_inc(x_turned, 1)
            pe.wait_ge(tables_landed, 16 * TABLES)
            for t in range(WT):
                turn(D[1][:, 0, t * 64:t * 64 + V_ROWS], vecs[:, t * P:(t + 1) * P], ident[0:V_ROWS, 0:V_ROWS])
            turn(D[1][:, 1, 0:3 * KT], g_rows[:, :], ident[0:3 * KT, 0:3 * KT])
            for n in range(2):
                ins = turn(D[1][:, 1, 64 + n * CMP:64 + (n + 1) * CMP],
                           wc_rows[:, n, :, :].rearrange("p h d -> p (h d)"), ident[0:CMP, 0:CMP])
            ins.then_inc(tables_turned, 1)
            pe.wait_ge(x_evac, 2 * KT)
            norm_sums(0)
            pe.wait_ge(tables_evac, 3)
            dense(0, 0, KT, hH, hL, ready=lambda k: pe.wait_ge(norm_lo, k + 1))
            dense(1, 1, KT, hH, hL)
            with pe.Fori(1, 3) as i:
                for b in range(2):
                    dense(2 * i + b, b, KT, hH, hL)
            pe.wait_ge(xc_ready, 2 * WT)
            pe.wait_ge(wg_landed, 64)
            for g in range(2 * WT):
                if g >= 2:
                    pe.wait_ge(gate_tanh, g - 1)
                product(E[:, 2 * (g % 2):2 * (g % 2) + 2, :], wg[:, g // WT, g % WT, :], xc[:, g % WT, :], True, True)\
                    .then_inc(gate_mm, 1)
            with pe.Fori(3, 5) as i:
                for b in range(2):
                    dense(2 * i + b, b, KT, hH, hL)
            pe.wait_ge(gate_tanh, 2 * WT)
            for t in range(WT):
                turn(E[0:2 + NS, 0, t * P:(t + 1) * P], eu[:, t, SEQ:2 + T], ident[:, :])
            for t in range(WT):
                ins = turn(E[0:3 + NS, 1, t * P:(t + 1) * P], exl[:, t, SEQ:3 + T], ident[:, :])
            ins.then_inc(tails_turned, 1)
            pe.wait_ge(v_lo, WT)
            with pe.Fori(C_MIX1 // 2, C_MIX2 // 2) as i:
                dense(2 * i, 0, KT, hH, hL)
                dense(2 * i + 1, 1, WT, vH, vL)
            pe.wait_ge(h_ready, WT + 2)
            for t in range(WT):
                ins = turn(E[0:1 + NS, 2, t * P:(t + 1) * P], t0[:, t, SEQ - 1:T], ident[:, :])
            ins.then_inc(tails_turned, 1)
            pe.wait_ge(lr_lo, 1)
            with pe.Fori(C_MIX2 // 2, C_Q // 2) as i:
                dense(2 * i, 0, KT, hH, hL)
                dense(2 * i + 1, 1, WT, lrH, lrL)
            with pe.Fori(C_Q // 2, C_KV // 2) as i:
                for b in range(2):
                    dense(2 * i + b, b, KT, hH, hL)
            pe.wait_ge(wt_lo, 1)
            pe.wait_ge(tails_evac, 3)
            for k in range(KT):
                product(E[:, 2:4, :], wtH[:, k, :], hH[:, k, :], k == 0, False)
                product(E[:, 2:4, :], wtH[:, k, :], hL[:, k, :], False, False)
                ins = product(E[:, 2:4, :], wtL[:, k, :], hH[:, k, :], False, k == KT - 1)
            ins.then_inc(gnsa_mm, 1)
            with pe.Fori(C_KV // 2, C_GM0 // 2) as i:
                for b in range(2):
                    dense(2 * i + b, b, KT, hH, hL)
            pe.wait_ge(gnsa_tanh, 1)
            gT = rstd[0:48, :]
            for q in range(QT):
                turn(E[:, 0, q * 48:(q + 1) * 48], gT[:, q * P:(q + 1) * P], ident[0:48, 0:48])
            turn(E[0:NS, 1, 0:48], gT[:, SEQ:T], ident[0:48, 0:48]).then_inc(gnsa_turned, 1)
            pe.wait_ge(cmp_sums, 2)
            for f in range(2):
                ins = turn(E[0:NBLK, 2, f * P:(f + 1) * P], kc_sum[:, 2 + f, :], ident[:, :])
            ins.then_inc(vc_turned, 1)
            pe.wait_ge(gates_ready, 2)
            csv = E[:, 0, :].rearrange("p (q f j r k) -> p q f r j k", q=QT, f=2, j=2, r=R)
            for q in range(QT):
                for t in range(KT):
                    ins = mm(csv[:, q, t // R, t % R, :, :], qT[:, t, q * P:(q + 1) * P],
                             kc_blk[:, t // R, :].rearrange("p (j k) -> p j k", j=2), start=True, stop=True)
            ins.then_inc(cmp_scores, 1)
            pe.wait_ge(vc_evac, 1)
            mm(E[:, 3, 0:KVC], rep[:, :, :].rearrange("p h k -> p (h k)"), tmp[0:NBLK, 1, 0:KVC],
               start=True, stop=True).then_inc(vc_rep, 1)
            with pe.Fori(C_GM0 // 2, C_NSA // 2) as i:
                for b in range(2):
                    dense(2 * i + b, b, KT, hH, hL)
            pe.wait_ge(cmp_prob, 1)
            for q in range(QT):
                ins = turn(E[:, 0, q * P:(q + 1) * P], th[:, 1, q * P:(q + 1) * P], ident[:, :])
            ins.then_inc(pc_turned, 1)
            places = [(vT, 0), (vT, 2), (kT, 0), (vT, 4), (kT, 2), (vT, 6)]
            for n in range(12):
                buf, o = places[n // 2]
                t = o + n % 2
                if n == 2:
                    pe.wait_ge(pc_evac, 1)
                if n >= 3:
                    pe.wait_ge(kv_evac, n - 2)
                if n == 0:
                    pe.wait_ge(vbig_ready, 1)
                elif n % 4 == 0:
                    pe.wait_ge(kvs_evac, n // 4)
                for q in range(QT):
                    turn(E[:, (n + 1) % 3, q * P:(q + 1) * P], buf[:, t, q * P:(q + 1) * P], ident[:, :])
                turn(E[0:NS, 3, (n % 4) * P:(n % 4 + 1) * P], buf[:, t, SEQ:T], ident[:, :]).then_inc(kv_turned, 1)
            pe.wait_ge(pc_evac, 1)
            for m in range(2):
                pe.wait_ge(tile_free[m], 1 + C_NSA)
            for q in range(QT):
                if q >= 2:
                    pe.wait_ge(cmp_evac, q - 1)
                for a in range(2):
                    ins = mm(D[q % 2][:, a, :], pcT[:, q, :], vbig[:, a * 512:(a + 1) * 512], start=True, stop=True)
                ins.then_inc(cmp_out, 1)
            pe.wait_ge(kv_evac, 12)
            pe.wait_ge(kvs_evac, 3)
            with pe.Fori(0, 2) as f:
                for v in range(64 + 3):
                    if v < 64:
                        rp, tt, j, a, qi = v // 32, (v // 16) % 2, (v // 8) % 2, (v // 4) % 2, v % 4
                        rows = slice(j * DH, (j + 1) * DH)
                        n = (qi + 1) * P
                        if v % 32 == 0:
                            pe.wait_ge(staged, 8 * f + 4 * rp + 4)
                        pe.wait_ge(exp_done, 64 * f + v + 1)
                        mm(E[:, v % 4, 0:n], q_st[rp][tt][rows, qi * P:n], k_st[rp][a][rows, 0:n], start=True, stop=False)
                        mm(E[:, v % 4, qi * P:n], ident_r[:, :], causal_r[:, :], start=False, stop=True)\
                            .then_inc(scores_done, 1)
                    if v == 2:
                        pe.wait_ge(cmp_evac, QT)
                    if 2 <= v < 66:
                        w = v - 2
                        pe.wait_ge(exp_done, 64 * f + w + 1 + 4)
                        pe.wait_ge(probT_done, 64 * f + w + 1)
                        for k in range(w % 4 + 1):
                            ins = turn(D[0][:, w % 2, k * P:(k + 1) * P], prob[w % 4][:, k * P:(k + 1) * P],
                                       ident[:, :])
                        ins.then_inc(probs_turned, 1)
                    if v >= 3:
                        w = v - 3
                        g, qi = w // 4, w % 4
                        j, a = (g // 2) % 2, g % 2
                        pe.wait_ge(probT_done, 64 * f + w + 1 + 2)
                        if qi == 0:
                            pe.wait_ge(o_added, 16 * f + g + 1)
                        for k in range(qi + 1):
                            ins = mm(D[1][:, g % 2, qi * DH:(qi + 1) * DH], probT[w % 2][:, k, :],
                                     kv_tok[:, k, 2 * a + 1, bass.ds((2 * f + j) * DH, DH)],
                                     start=(k == 0), stop=(k == qi))
                        ins.then_inc(pv_done, 1)

            pe.wait_ge(qpad_ready, 8)
            for s in range(NS):
                pe.wait_ge(s_prod, s + 1)
                for f in range(2):
                    for g in range(NPG):
                        o = (s * 2 + f) * NBLK_S + 2 * g
                        ins = mm(E[:, 0, o:o + 2], prod[s % 2][:, g, 2 * f:2 * f + 2, :].rearrange("p g d -> p (g d)"),
                                 blkpad[:, 0, 0:2], start=True, stop=True)
                ins.then_inc(s_kc_mm, 1)
            for s in range(NS):
                pe.wait_ge(s_prod, NS + s + 1)
                if s >= 2:
                    pe.wait_ge(s_vc_evac, s - 1)
                for g in range(NPG):
                    ins = mm(E[0:NBLK_S, 1 + s % 2, 0:KVC], blkpad[:, g, :],
                             prod[s % 2][:, g, :, :].rearrange("p g d -> p (g d)"), start=(g == 0), stop=(g == NPG - 1))
                ins.then_inc(s_vc_mm, 1)
            for y in range(3):
                if y == 0:
                    pe.wait_ge(s_kc_evac, 1)
                    for s in range(NS):
                        for f in range(2):
                            ins = mm(E[:, 3, 0:NBLK_S], q_pad[:, s, f, :], kcs[:, s, f, :],
                                     start=(s == 0 and f == 0), stop=(s == NS - 1 and f == 1))
                    ins.then_inc(s_scores, 1)
                else:
                    if y == 1:
                        pe.wait_ge(s_vc_evac, NS)
                    pe.wait_ge(s_nmax, y)
                    for s in range(NS + 1):
                        if s < NS:
                            pe.wait_ge(slot_landed[s], 32 * (2 * y + 1) if y == 1 else 32 * 4 + 16)
                            if y == 2 or s >= 2:
                                pe.wait_ge(s_k_evac, (y - 1) * NS + s - 1)
                            for f in range(2):
                                for g in range(NPG):
                                    o = f * PAST + g * P
                                    ins = turn(E[:, s % 2, o:o + P], slot[s][:, g, f * P:(f + 1) * P], ident[:, :])
                            ins.then_inc(s_k_turned, 1)
                        if s > 0:
                            r = s - 1
                            pe.wait_ge(s_k_evac, (y - 1) * NS + s)
                            for f in range(2):
                                ins = mm(E[:, 2, 0:PAST], q_pad[:, r, f, :], kTs[r % 2][:, f, :],
                                         start=(r == 0 and f == 0), stop=(r == NS - 1 and f == 1))
                            ins.then_inc(s_k_used, 1)
                    for f in range(2):
                        ins = mm(E[:, 3, 0:NS], q_all[:, f, :], kT[:, 2 * (y - 1) + f, SEQ:T],
                                 start=(f == 0), stop=(f == 1))
                    ins.then_inc(s_scores, 1)
                pe.wait_ge(s_exp, y + 1)
                if y == 0:
                    turn(D[0][0:NBLK_S, 0, 0:P], p_sb[:, 0:NBLK_S], ident[:, :]).then_inc(s_p_turned, 1)
                    pe.wait_ge(s_vc_evac, NS)
                    pe.wait_ge(s_pT, 1)
                    for s in range(NS):
                        ins = mm(D[1][:, 0, 0:KVC], pT_cmp[:, s, :], vcs[:, s, :], start=(s == 0), stop=(s == NS - 1))
                    ins.then_inc(s_out, 1)
                else:
                    for g in range(NPG):
                        turn(D[0][:, 0, g * P:(g + 1) * P], p_sb[:, g * P:(g + 1) * P], ident[:, :])
                    turn(D[0][0:NS, 1, 0:P], p_sb[:, PAST:PAST + NS], ident[:, :]).then_inc(s_p_turned, 1)
                    pe.wait_ge(s_pT, 3 * y + 1)
                    pe.wait_ge(s_sel, y)
                    mm(D[1][:, 0, 0:KVC], pT_new[:, :], kvs_tok[:, 2 * y - 1, :], start=True, stop=False)
                    for s in range(NS):
                        pe.wait_ge(slot_landed[s], 32 * 4 if y == 1 else 32 * 4 + 32)
                        for g in range(NPG):
                            ins = mm(D[1][:, 0, 0:KVC], pT_pad[:, g, s, :], slot[s][:, g, :],
                                     start=False, stop=(s == NS - 1 and g == NPG - 1))
                        ins.then_inc(s_v_used if s < NS - 1 else s_out, 1)
            pe.wait_ge(s_sel, 4)
            turn(D[1][:, 1, 0:P], o_sum, ident[:, :]).then_inc(os_turned, 1)
            for ft in range(KT):
                if ft >= 4:
                    pe.wait_ge(on_lo, ft - 3)
                for q in range(QT):
                    ins = turn(E[:, ft % 4, q * P:(q + 1) * P], onsa[:, q, ft * P:(ft + 1) * P], ident[:, :])
                ins.then_inc(on_turned, 1)
            pe.wait_ge(ons_lo, 2)
            dense(C_NSA, 0, KT, onH, onL, ready=lambda k: pe.wait_ge(on_lo, k + 1))
            dense(C_NSA + 1, 1, KT, onH, onL)
            with pe.Fori(C_NSA // 2 + 1, C_WO // 2) as i:
                for b in range(2):
                    dense(2 * i + b, b, KT, onH, onL)
            dense(C_WO, 0, KT, hH, hL, ready=lambda k: pe.wait_ge(mix_lo, k + 1))
            dense(C_WO + 1, 1, KT, hH, hL)
            with pe.Fori(C_WO // 2 + 1, C_FI // 2) as i:
                for b in range(2):
                    dense(2 * i + b, b, KT, hH, hL)
            norm_sums(1)
            dense(C_FI, 0, KT, hH, hL, ready=lambda k: pe.wait_ge(norm_lo, KT + k + 1))
            dense(C_FI + 1, 1, KT, hH, hL)
            with pe.Fori(C_FI // 2 + 1, C_FO // 2) as i:
                for b in range(2):
                    dense(2 * i + b, b, KT, hH, hL)
            for m in range(2):
                pe.wait_ge(tile_free[m], 1 + C_FO)
            pe.wait_ge(act_lo, 2 + FT)
            with pe.Fori(0, 2) as i:
                for j in range(6):
                    if j % 3 == 0:
                        pe.wait_ge(x_last, 4 * i + 2 + 2 * (j // 3))
                    outs = [D[0], D[1]] if j < 3 else [E[:, 0:2, :], E[:, 2:4, :]]
                    nk = KT if j % 3 < 2 else FT - 2 * KT
                    dense(6 * i + C_FO + j, j % 2, nk, actH, actL, x0=(j % 3) * KT, outs=outs,
                          first=(j % 3 == 0), last=(j % 3 == 2))
            norm_sums(2)
            for q in range(QT):
                if q == 0:
                    pe.wait_ge(y_ready, KT)
                if q >= 2:
                    pe.wait_ge(y_evac_a, q - 1)
                    pe.wait_ge(y_evac_v, q - 1)
                for ft in range(KT):
                    ins = turn(D[q % 2][:, ft // 4, (ft % 4) * P:(ft % 4 + 1) * P], yT[:, ft, q * P:(q + 1) * P],
                               ident[:, :])
                ins.then_inc(y_turned, 1)
            for ft in range(KT):
                ins = turn(E[0:NS, ft // 4, (ft % 4) * P:(ft % 4 + 1) * P], yT[:, ft, SEQ:T], ident[:, :])
            ins.then_inc(y_turned, 1)


_INS = ["x_prompt", "x_sample", "cache_kv", "cache_win", "state_sconv", "state_lru_conv", "state_lru_h", "page_table",
        "norm1_g", "w_in", "w_cmp_k", "w_cmp_v", "w_nsa_out", "w_sc_conv", "w_sc_out", "w_lru_conv", "b_lru_conv",
        "w_lru_gate", "b_lru_gate", "lru_lambda", "w_lru_out", "w_o", "norm2_g", "w_ffn_in", "w_ffn_out", "final_g"]
_OUTS = [("y_prompt", (1, SEQ, D_MODEL)), ("y_sample", (NS, 1, D_MODEL)), ("kv_p", (1, 1, SEQ, 4, N_KV, DH)),
         ("win_p", (1, 1, SEQ, 2, N_KV, DH)), ("sconv_p", (1, 1, 2, WID)), ("lruconv_p", (1, 1, 3, WID)),
         ("lruh_p", (1, 1, WID)), ("kv_s", (1, NS, 1, 4, N_KV, DH)), ("win_s", (1, NS, PAST, 2, N_KV, DH)),
         ("sconv_s", (1, NS, 2, WID)), ("lruconv_s", (1, NS, 3, WID)), ("lruh_s", (1, NS, WID))]


def kernel(**inputs):
    import numpy as np
    import concourse.bacc as bacc
    from concourse.bass_utils import run_bass_kernel_spmd

    nc = bacc.Bacc("TRN2", target_bir_lowering=False, num_devices=1)
    arrays, args = {}, []
    for name in _INS:
        a = np.ascontiguousarray(inputs[name])
        arrays[f"in_{name}"] = a
        args.append(nc.dram_tensor(f"in_{name}", a.shape, mybir.dt.from_np(a.dtype), kind="ExternalInput").ap())
    for name, shape in _OUTS:
        args.append(nc.dram_tensor(f"out_{name}", shape, F32, kind="ExternalOutput").ap())
    build(nc, *args)
    r = run_bass_kernel_spmd(nc, [arrays], core_ids=[0])
    return tuple(r.results[0][f"out_{name}"] for name, _ in _OUTS)
```
